# Optimizing a Trainium2 kernel written in Bass

```python
import math
import jax, jax.numpy as jnp
from jax import lax
import numpy as np

D_MODEL = 1024
BATCH = 1
SEQ = 1024
DEPTH = 2

HEAD_DIM = 64
A_HEADS = D_MODEL // 4 // HEAD_DIM
A_WIDTH = A_HEADS * HEAD_DIM
B_HEADS = D_MODEL // 2 // (2 * HEAD_DIM)
B_QK = B_HEADS * 2 * HEAD_DIM
B_V = B_HEADS * 2 * HEAD_DIM
C_WIDTH = D_MODEL // 4
MIX_WIDTH = A_WIDTH + B_V + C_WIDTH
IN_COLS = 3 * A_WIDTH + 2 * B_QK + B_V + 3 * C_WIDTH
SPLITS = (A_WIDTH, 2 * A_WIDTH, 3 * A_WIDTH,
          3 * A_WIDTH + B_QK, 3 * A_WIDTH + 2 * B_QK, 3 * A_WIDTH + 2 * B_QK + B_V,
          3 * A_WIDTH + 2 * B_QK + B_V + C_WIDTH, 3 * A_WIDTH + 2 * B_QK + B_V + 2 * C_WIDTH)
DILATED_PATTERNS = ((128, 1), (512, 4), (2048, 16))
Q_BLOCK = 128
CONV_WIDTH = 3
D_FF = ((8 * D_MODEL // 3 + 127) // 128) * 128
ROPE_THETA = 500000.0
ROPE_FRACTION = 4
NORM_EPS = 1e-6
SUBLN_EPS = 1e-5

kernel_name = "hybrid_dilated_diffattn_shortconv_block"

def rms_norm(x, g, eps=NORM_EPS):
    xf = x.astype(jnp.float32)
    y = xf * lax.rsqrt(jnp.mean(xf * xf, axis=-1, keepdims=True) + eps)
    return (y * g.astype(jnp.float32)).astype(x.dtype)

def partial_rope(x, pos):
    e = x.shape[-1]
    r = e // ROPE_FRACTION
    half = r // 2
    inv = ROPE_THETA ** (-(jnp.arange(half, dtype=jnp.float32) * 2.0 / r))
    ang = pos.astype(jnp.float32)[..., None] * inv
    cos = jnp.cos(ang)[:, :, None, :]
    sin = jnp.sin(ang)[:, :, None, :]
    xr = x[..., :r].astype(jnp.float32)
    x1, x2 = xr[..., :half], xr[..., half:]
    rot = jnp.concatenate([x1 * cos - x2 * sin, x1 * sin + x2 * cos], axis=-1).astype(x.dtype)
    return jnp.concatenate([rot, x[..., r:]], axis=-1)

def causal_dwconv(x, w):
    c = x.shape[-1]
    return lax.conv_general_dilated(
        x, w.astype(x.dtype)[:, None, :], window_strides=(1,),
        padding=[(CONV_WIDTH - 1, 0)], dimension_numbers=('NWC', 'WIO', 'NWC'),
        feature_group_count=c)

def dilated_window_branch(q, k, v, window, dilation):
    b, s, h, e = q.shape
    steps = window // dilation
    L = s // dilation
    nblk = -(-L // steps)
    Lp = nblk * steps

    def to_blocks(t):
        t = t.reshape(b, L, dilation, h, t.shape[-1]).transpose(0, 2, 3, 1, 4)
        t = jnp.pad(t, ((0, 0), (0, 0), (0, 0), (0, Lp - L), (0, 0)))
        return t.reshape(b, dilation, h, nblk, steps, t.shape[-1])

    def with_prev(t):
        prev = jnp.pad(t, ((0, 0), (0, 0), (0, 0), (1, 0), (0, 0), (0, 0)))[:, :, :, :-1]
        return jnp.concatenate([prev, t], axis=4)

    qb = to_blocks(q)
    kc = with_prev(to_blocks(k))
    vc = with_prev(to_blocks(v))
    sc = jnp.einsum('brhnqe,brhnke->brhnqk', qb, kc, preferred_element_type=jnp.float32)
    qi = jnp.arange(steps)[:, None]
    kj = jnp.arange(2 * steps)[None, :]
    dist = qi + steps - kj
    key_idx = jnp.arange(nblk)[:, None, None] * steps + kj - steps
    valid = (dist >= 0) & (dist <= steps) & (key_idx >= 0)
    sc = jnp.where(valid, sc, -jnp.inf)
    m = jnp.max(sc, axis=-1, keepdims=True)
    p = jnp.exp(sc - m)
    l = jnp.sum(p, axis=-1, keepdims=True)
    o = jnp.einsum('brhnqk,brhnke->brhnqe', p, vc) / l

    def from_blocks(t):
        f = t.shape[-1]
        t = t.reshape(b, dilation, h, Lp, f)[:, :, :, :L]
        return t.transpose(0, 3, 1, 2, 4).reshape(b, s, h, f)

    return from_blocks(o), from_blocks(m), from_blocks(l)

def dilated_mixture_attention(q, k, v):
    outs = [dilated_window_branch(q, k, v, w, d) for (w, d) in DILATED_PATTERNS]
    m_all = outs[0][1]
    for _, m_i, _ in outs[1:]:
        m_all = jnp.maximum(m_all, m_i)
    num = 0.0
    den = 0.0
    for o_i, m_i, l_i in outs:
        w_i = l_i * jnp.exp(m_i - m_all)
        num = num + w_i * o_i
        den = den + w_i
    return num / den

def differential_attention(q1, q2, k1, k2, v, lam):
    b, s, h, e = q1.shape
    nqb = s // Q_BLOCK
    kpos = jnp.arange(s)

    def blocks(t):
        return t.reshape(b, nqb, Q_BLOCK, h, t.shape[-1]).transpose(1, 0, 2, 3, 4)

    def one_block(args):
        q1b, q2b, i = args
        qpos = i * Q_BLOCK + jnp.arange(Q_BLOCK)
        causal = kpos[None, :] <= qpos[:, None]

        def attn(qb, kk):
            sc = jnp.einsum('bqhe,bkhe->bhqk', qb, kk, preferred_element_type=jnp.float32)
            return jax.nn.softmax(jnp.where(causal, sc, -jnp.inf), axis=-1)

        a = attn(q1b, k1) - lam * attn(q2b, k2)
        return jnp.einsum('bhqk,bkhe->bqhe', a, v)

    o = lax.map(one_block, (blocks(q1), blocks(q2), jnp.arange(nqb)))
    return o.transpose(1, 0, 2, 3, 4).reshape(b, s, h, v.shape[-1])

def hybrid_mixer(h, pos, w_in, lq1, lk1, lq2, lk2, subln_g, conv_w, w_out, layer_idx):
    b, s, _ = h.shape
    proj = h @ w_in
    aq, ak, av, bq, bk, bv, cb, cc, ch = jnp.split(proj, SPLITS, axis=-1)
    scale = HEAD_DIM ** -0.5

    aq = partial_rope(aq.reshape(b, s, A_HEADS, HEAD_DIM), pos) * scale
    ak = partial_rope(ak.reshape(b, s, A_HEADS, HEAD_DIM), pos)
    av = av.reshape(b, s, A_HEADS, HEAD_DIM)
    o_a = dilated_mixture_attention(aq, ak, av).astype(h.dtype).reshape(b, s, A_WIDTH)

    bq = bq.reshape(b, s, B_HEADS, 2, HEAD_DIM)
    bk = bk.reshape(b, s, B_HEADS, 2, HEAD_DIM)
    q1 = partial_rope(bq[:, :, :, 0], pos) * scale
    q2 = partial_rope(bq[:, :, :, 1], pos) * scale
    k1 = partial_rope(bk[:, :, :, 0], pos)
    k2 = partial_rope(bk[:, :, :, 1], pos)
    bv = bv.reshape(b, s, B_HEADS, 2 * HEAD_DIM)
    lam_init = 0.8 - 0.6 * math.exp(-0.3 * layer_idx)
    lam = (jnp.exp(jnp.sum(lq1.astype(jnp.float32) * lk1.astype(jnp.float32)))
           - jnp.exp(jnp.sum(lq2.astype(jnp.float32) * lk2.astype(jnp.float32))) + lam_init)
    o_b = differential_attention(q1, q2, k1, k2, bv, lam)
    o_b = rms_norm(o_b, subln_g, SUBLN_EPS) * (1.0 - lam_init)
    o_b = o_b.astype(h.dtype).reshape(b, s, B_V)

    o_c = cb * causal_dwconv(cc * ch, conv_w)

    return jnp.concatenate([o_a, o_b, o_c], axis=-1) @ w_out

def conv_glu_ffn(h, w_up, conv_w, w_down):
    gu = h @ w_up
    g, u = jnp.split(gu, 2, axis=-1)
    g = causal_dwconv(g, conv_w)
    return (jax.nn.silu(g) * u) @ w_down

def setup_inputs(seed: int = 0) -> dict:
    key = jax.random.key(seed)
    ks = jax.random.split(key, 16)

    def nrm(k, shape, scale):
        return jax.random.normal(k, shape, jnp.float32) * scale

    return {
        "x": nrm(ks[0], (BATCH, SEQ, D_MODEL), 1.0),
        "positions": jnp.tile(jnp.arange(SEQ, dtype=jnp.int32)[None, :], (BATCH, 1)),
        "norm_mix_g": 1.0 + nrm(ks[1], (DEPTH, D_MODEL), 0.05),
        "w_in": nrm(ks[2], (DEPTH, D_MODEL, IN_COLS), D_MODEL ** -0.5),
        "lambda_q1": nrm(ks[3], (DEPTH, HEAD_DIM), 0.1),
        "lambda_k1": nrm(ks[4], (DEPTH, HEAD_DIM), 0.1),
        "lambda_q2": nrm(ks[5], (DEPTH, HEAD_DIM), 0.1),
        "lambda_k2": nrm(ks[6], (DEPTH, HEAD_DIM), 0.1),
        "subln_g": 1.0 + nrm(ks[7], (DEPTH, 2 * HEAD_DIM), 0.05),
        "conv_mix_w": nrm(ks[8], (DEPTH, CONV_WIDTH, C_WIDTH), CONV_WIDTH ** -0.5),
        "w_out": nrm(ks[9], (DEPTH, MIX_WIDTH, D_MODEL), MIX_WIDTH ** -0.5),
        "norm_ffn_g": 1.0 + nrm(ks[10], (DEPTH, D_MODEL), 0.05),
        "w_up": nrm(ks[11], (DEPTH, D_MODEL, 2 * D_FF), D_MODEL ** -0.5),
        "conv_ffn_w": nrm(ks[12], (DEPTH, CONV_WIDTH, D_FF), CONV_WIDTH ** -0.5),
        "w_down": nrm(ks[13], (DEPTH, D_FF, D_MODEL), D_FF ** -0.5),
        "final_g": 1.0 + nrm(ks[14], (D_MODEL,), 0.05),
    }

def reference(x, positions, norm_mix_g, w_in, lambda_q1, lambda_k1, lambda_q2, lambda_k2,
              subln_g, conv_mix_w, w_out, norm_ffn_g, w_up, conv_ffn_w, w_down, final_g):
    h = x
    for layer in range(DEPTH):
        hn = rms_norm(h, norm_mix_g[layer])
        h = h + hybrid_mixer(hn, positions, w_in[layer], lambda_q1[layer], lambda_k1[layer],
                             lambda_q2[layer], lambda_k2[layer], subln_g[layer],
                             conv_mix_w[layer], w_out[layer], layer)
        hn = rms_norm(h, norm_ffn_g[layer])
        h = h + conv_glu_ffn(hn, w_up[layer], conv_ffn_w[layer], w_down[layer])
    return rms_norm(h, final_g)


_drawn_inputs = setup_inputs


def setup_inputs(seed=0):
    import zlib

    import numpy as np

    out = dict(_drawn_inputs(seed))
    spreads = {}
    factors = {}
    for name, (base, spread) in spreads.items():
        noise = np.random.default_rng([zlib.crc32(name.encode()), seed]).standard_normal(out[name].shape)
        drawn = base * np.exp(spread * noise) if base else spread * noise
        out[name] = __import__('jax').numpy.asarray(drawn.astype(out[name].dtype))
    for name, factor in factors.items():
        out[name] = (out[name] * factor).astype(out[name].dtype)
    return out
```

```python
import math
from contextlib import ExitStack

import numpy as np

import concourse.bass as bass
import concourse.mybir as mybir

P = 128
D_MODEL = 1024
SEQ = 1024
DEPTH = 2
HEAD_DIM = 64
A_UNITS = D_MODEL // 4 // P
B_UNITS = D_MODEL // 2 // P
C_UNITS = D_MODEL // 4 // P
D_FF = ((8 * D_MODEL // 3 + 127) // 128) * 128
F_TILES = D_FF // P
KT = D_MODEL // P
QB = SEQ // P
HALF = 512
TAPS = 3
DILATED = ((128, 1), (512, 4), (2048, 16))
ROPE_DIMS = HEAD_DIM // 4
ROPE_THETA = 500000.0
NORM_EPS, SUBLN_EPS = 1e-6, 1e-5
SCALE = HEAD_DIM ** -0.5
NEG = -1e30

MIX_UNITS = A_UNITS + B_UNITS + C_UNITS
LAYER_TILES = 4 * MIX_UNITS + 3 * F_TILES
TILES = DEPTH * LAYER_TILES
W_SLOTS = 2

V_FFN_G, V_NEXT_G = 0, KT
V_CONV_MIX = 2 * KT
V_CONV_FFN = V_CONV_MIX + TAPS * C_UNITS
V_SUBLN = V_CONV_FFN + TAPS * F_TILES
V_LAMBDA = V_SUBLN + 1
V_LAM_INIT = V_LAMBDA + 4
V_ONE_LESS = V_LAM_INIT + 1
V_NEG_LAM = V_ONE_LESS + 1
V_SUBLN_SCALED = V_NEG_LAM + 1
NV = V_SUBLN_SCALED + 1

TWO_PI = 2 * math.pi
TURN_A = 6.28125
TURN_B = float(np.float32(int((TWO_PI - TURN_A) * 2 ** 20) / 2 ** 20))
TURN_C = TWO_PI - TURN_A - TURN_B
ROUNDER = 1.5 * 2 ** 23
SIN_END = 3.1415925


class Seen:

    def __init__(self):
        self.count = {}

    def __call__(self, semaphore, n=1):
        self.count[semaphore] = self.count.get(semaphore, 0) + n
        return self.count[semaphore]

    def settle(self, engine):
        for semaphore, n in self.count.items():
            if n:
                engine.wait_ge(semaphore, n).then_inc(semaphore, -n)
                self.count[semaphore] = 0


def build(nc, x_t, positions, stream, vectors, first_g, columns, square, masks, out_t):
    f32, f32r, bf16, i32 = (mybir.dt.float32, mybir.dt.float32r, mybir.dt.bfloat16, mybir.dt.int32)
    ALU, ACT = mybir.AluOpType, mybir.ActivationFunctionType
    ctx = ExitStack()
    with ctx:
        def sbuf(name, shape, dtype=f32):
            return ctx.enter_context(nc.sbuf_tensor(name, shape, dtype))

        def sem(name):
            return ctx.enter_context(nc.semaphore(name))

        h = sbuf("h", [P, KT, SEQ])
        x_hi = sbuf("x_hi", [P, KT, SEQ], f32r)
        x_lo = sbuf("x_lo", [P, KT, SEQ], f32r)
        stage = sbuf("stage", [P, W_SLOTS, D_MODEL])
        w_hi = sbuf("w_hi", [P, W_SLOTS, D_MODEL], f32r)
        w_lo = sbuf("w_lo", [P, W_SLOTS, D_MODEL], f32r)
        mix_hi = sbuf("mix_hi", [P, SEQ], f32r)
        mix_lo = sbuf("mix_lo", [P, SEQ], f32r)
        q_cur, k_cur = sbuf("q_cur", [P, SEQ]), sbuf("k_cur", [P, SEQ])
        v_cur = sbuf("v_cur", [P, QB, P])
        q_next, k_next = sbuf("q_next", [P, SEQ]), sbuf("k_next", [P, SEQ])
        v_next = sbuf("v_next", [P, SEQ])
        shuffled = sbuf("shuffled", [P, SEQ])
        prob = sbuf("prob", [P, 2, 2, SEQ])
        prob_t = sbuf("prob_t", [P, 2, HALF])
        heads = sbuf("heads", [P, SEQ])
        rstd_all = sbuf("rstd_all", [P, SEQ])
        padded = sbuf("padded", [P, TAPS - 1 + SEQ])
        cos_t, sin_t = sbuf("cos_t", [P, SEQ]), sbuf("sin_t", [P, SEQ])
        eye, ones = sbuf("eye", [P, P]), sbuf("ones", [P, P])
        mask = sbuf("mask", [P, 3, SEQ], bf16)
        vec = sbuf("vec", [P, DEPTH, NV])
        lay = sbuf("lay", [P, NV])
        g0 = sbuf("g0", [P, KT])
        col = sbuf("col", [P, 2])
        taps = sbuf("taps", [P, 2 * TAPS])
        lam = sbuf("lam", [P, 2 * DEPTH])
        lam_exp = sbuf("lam_exp", [P, 2 * DEPTH])
        top, neg_top = sbuf("top", [P, 2]), sbuf("neg_top", [P, 2])
        total, share = sbuf("total", [P, 2]), sbuf("share", [P, 2])
        rs = sbuf("rs", [P, 4, QB])
        ps = ctx.enter_context(nc.psum_tensor("ps", [P, 8, HALF], f32))

        turns, angle = q_next, k_next
        squares, square_sum = (q_cur, k_cur), heads
        diagonal, head_squares = prob[:, 0, 0, :], prob[:, 1, 1, :]

        def bank(b, n=1):
            return ps[:, b:b + n, :].rearrange("p b t -> p (b t)")

        PROJ, SCORE, TURNED, HEAD = 0, 2, 6, 7
        DOWN = SCORE

        stage_full = [sem(f"stage_full{s}") for s in range(W_SLOTS)]
        stage_free = sem("stage_free")
        w_ready, w_free = sem("w_ready"), sem("w_free")
        pool_seq = sem("pool_seq")
        consts_in, pos_in = sem("consts_in"), sem("pos_in")
        x_in = [sem(f"x_in{m}") for m in range(KT)]
        consts_pe = sem("consts_pe")
        dve_seq, act_seq = sem("dve_seq"), sem("act_seq")
        x_ready = sem("x_ready")
        half_done, half_free = sem("half_done"), sem("half_free")
        down_done, down_free = sem("down_done"), sem("down_free")
        mix_ready = sem("mix_ready")
        h_new, h_used = sem("h_new"), sem("h_used")
        sum_ready, sum_done = sem("sum_ready"), sem("sum_done")
        sq_ready = sem("sq_ready")
        diag_ready = sem("diag_ready")
        spread_act, spread_dve = sem("spread_act"), sem("spread_dve")
        rstd_ready = sem("rstd_ready")
        cur_ready = sem("cur_ready")
        next_ready, next_free = sem("next_ready"), sem("next_free")
        v_ready = sem("v_ready")
        score_done, score_free = sem("score_done"), sem("score_free")
        top_ready, exp_done = sem("top_ready"), sem("exp_done")
        prob_ready, prob_free = sem("prob_ready"), sem("prob_free")
        turned_done, turned_out = sem("turned_done"), sem("turned_out")
        head_done, head_free = sem("head_done"), sem("head_free")
        heads_ready = sem("heads_ready")
        value_ready, hi_ready = sem("value_ready"), sem("hi_ready")
        gate_ready, gate_used = sem("gate_ready"), sem("gate_used")
        conv_ready, silu_done = sem("conv_ready"), sem("silu_done")
        angle_ready, trig_done = sem("angle_ready"), sem("trig_done")
        lam_summed = sem("lam_summed")
        lam_exped = sem("lam_exped")
        out_ready, out_done = sem("out_ready"), sem("out_done")

        block = ctx.enter_context(nc.Block())

        @block.sync
        def _(sp):
            seen = Seen()
            for source, tile in ((vectors, vec[:, :, :].rearrange("p l v -> p (l v)")), (first_g, g0[:, :]),
                                 (columns, col[:, :]), (square, eye[:, :]),
                                 (masks, mask[:, :, :].rearrange("p m t -> p (m t)"))):
                sp.dma_start(tile, source).then_inc(consts_in, 16)
            rounds = stream.rearrange("(r s) p n -> r s p n", s=W_SLOTS)
            with sp.Fori(0, TILES // W_SLOTS) as r:
                for s in range(W_SLOTS):
                    sp.wait_ge(stage_free, seen(stage_free))
                    sp.dma_start(stage[:, s, :], rounds[bass.ds(r, 1), s, :, :].rearrange("o p n -> (o p) n"))\
                      .then_inc(stage_full[s], 16)
                seen.settle(sp)
            for m in range(KT):
                sp.wait_ge(out_ready, m + 1)
                sp.dma_start(out_t[m * P:(m + 1) * P, :], h[:, m, :]).then_inc(out_done, 16)
            sp.wait_ge(out_done, 16 * KT)

        @block.gpsimd
        def _(pool):
            seen = Seen()
            pool.sem_inc(stage_free, W_SLOTS)
            with pool.Fori(0, TILES // W_SLOTS):
                for s in range(W_SLOTS):
                    pool.wait_ge(stage_full[s], seen(stage_full[s], 16))
                    pool.wait_ge(w_free, seen(w_free))
                    pool.tensor_copy(w_hi[:, s, :], stage[:, s, :]).then_inc(pool_seq, 1)
                    pool.wait_ge(pool_seq, seen(pool_seq))
                    pool.tensor_tensor(w_lo[:, s, :], stage[:, s, :], w_hi[:, s, :].bitcast(f32), ALU.subtract)\
                        .then_inc(pool_seq, 1)
                    pool.wait_ge(pool_seq, seen(pool_seq))
                    pool.sem_inc(w_ready, 1)
                    pool.sem_inc(stage_free, 1)
                seen.settle(pool)

        @block.tensor
        def _(pe):
            seen = Seen()
            slot = [0]

            def next_slot():
                s = slot[0]
                slot[0] = (s + 1) % W_SLOTS
                return s

            def three_pass(out, slices, moving, start, stop):
                (s, w), (hi, lo) = slices, moving
                first = pe.matmul(out, w_hi[:, s, w], hi, start=start, stop=False)
                pe.matmul(out, w_hi[:, s, w], lo, start=False, stop=False)
                return first, pe.matmul(out, w_lo[:, s, w], hi, start=False, stop=stop)

            def project_half(s, n, first=False):
                t = slice(n * HALF, (n + 1) * HALF)
                if n == 0:
                    pe.wait_ge(w_ready, seen(w_ready))
                pe.wait_ge(half_free, seen(half_free))
                for k in range(KT):
                    if first and n == 0:
                        pe.wait_ge(x_ready, seen(x_ready))
                    begun, last = three_pass(bank(PROJ + n), (s, slice(k * P, (k + 1) * P)),
                                             (x_hi[:, k, t], x_lo[:, k, t]), k == 0, k == KT - 1)
                    if n == 0 and k == 0:
                        begun.then_inc(w_free, 1)
                last.then_inc(half_done, 1)

            def project(first=False):
                s = next_slot()
                for n in range(2):
                    project_half(s, n, first)

            def down():
                s = next_slot()
                pe.wait_ge(w_ready, seen(w_ready))
                pe.wait_ge(mix_ready, seen(mix_ready))
                for m in range(KT):
                    pe.wait_ge(down_free, seen(down_free))
                    for n in range(2):
                        t = slice(n * HALF, (n + 1) * HALF)
                        begun, last = three_pass(bank(DOWN + 2 * (m % 2) + n), (s, slice(m * P, (m + 1) * P)),
                                                 (mix_hi[:, t], mix_lo[:, t]), True, True)
                        if m == 0 and n == 0:
                            begun.then_inc(w_free, 1)
                    last.then_inc(down_done, 1)

            def sums(source, ready):
                pe.wait_ge(ready, seen(ready))
                for b in range(QB):
                    last = pe.matmul(ps[:, HEAD, b:b + 1], source[:, b * P:(b + 1) * P], ones[:, 0:1],
                                     start=True, stop=True)
                last.then_inc(sum_done, 1)

            def spread(done):
                pe.wait_ge(diag_ready, seen(diag_ready))
                for n in range(2):
                    last = pe.matmul(bank(SCORE + n), ones[:, :], diagonal[:, n * HALF:(n + 1) * HALF],
                                     start=True, stop=True)
                last.then_inc(done, 1)

            def start_normed():
                project(first=True)
                sums(square_sum, sum_ready)
                spread(spread_act)

            def scores(i):
                if i == 0:
                    pe.wait_ge(cur_ready, seen(cur_ready))
                pe.wait_ge(score_free, seen(score_free))
                keys = (i + 1) * P
                for j in range(2):
                    rows = slice(HEAD_DIM * j, HEAD_DIM * (j + 1))
                    for n in range(0, keys, HALF):
                        wide = min(HALF, keys - n)
                        last = pe.matmul(ps[:, SCORE + 2 * j + n // HALF, 0:wide], q_cur[rows, i * P:(i + 1) * P],
                                         k_cur[rows, n:n + wide], start=True, stop=True)
                last.then_inc(score_done, 1)

            def turn(source, blocks):
                for b in range(blocks):
                    last = pe.transpose(ps[:, TURNED, b * P:(b + 1) * P], source[:, b * P:(b + 1) * P], eye[:, :])
                last.then_inc(turned_done, 1)

            def attend(i, dilated):
                groups = [(j, b, min(4, i + 1 - b)) for j in range(2 if dilated else 1) for b in range(0, i + 1, 4)]
                pe.wait_ge(prob_ready, seen(prob_ready))
                pe.wait_ge(head_free, seen(head_free))
                turn(prob[:, i % 2, 0, :], groups[0][2])
                for n, (j, b0, blocks) in enumerate(groups):
                    pe.wait_ge(turned_out, seen(turned_out))
                    if n + 1 < len(groups):
                        jn, bn, more = groups[n + 1]
                        turn(prob[:, i % 2, jn, bn * P:], more)
                    for b in range(b0, b0 + blocks):
                        dims = slice(HEAD_DIM * j, HEAD_DIM * (j + 1)) if dilated else slice(0, P)
                        last = pe.matmul(ps[dims, HEAD, 0:P], v_cur[:, b, dims],
                                         prob_t[:, n % 2, (b - b0) * P:(b - b0 + 1) * P],
                                         start=b == 0, stop=b == i)
                last.then_inc(head_done, 1)

            def turn_v():
                pe.wait_ge(v_ready, seen(v_ready))
                for g in range(2):
                    turn(v_next[:, g * HALF:], 4)
                    pe.wait_ge(turned_out, seen(turned_out))

            def unit(dilated, next_attends=True):
                s = None
                for i in range(QB):
                    scores(i)
                    if i:
                        attend(i - 1, dilated)
                    if i >= QB - 4:
                        n = i % 2
                        s = next_slot() if n == 0 else s
                        project_half(s, n)
                attend(QB - 1, dilated)
                s = next_slot()
                project_half(s, 0)
                if not dilated:
                    sums(head_squares, sq_ready)
                project_half(s, 1)
                if not dilated:
                    spread(spread_dve)
                if next_attends:
                    turn_v()
                down()

            pe.wait_ge(consts_pe, seen(consts_pe))
            pe.matmul(ps[:, TURNED, 0:2 * DEPTH], ones[:, :], lam[:, :], start=True, stop=True).then_inc(lam_summed, 1)
            seen.settle(pe)
            with pe.Fori(0, DEPTH):
                start_normed()
                project()
                project()
                turn_v()
                seen.settle(pe)
                with pe.Fori(0, A_UNITS):
                    unit(True)
                    seen.settle(pe)
                with pe.Fori(0, B_UNITS - 1):
                    unit(False)
                    seen.settle(pe)
                unit(False, next_attends=False)
                for _ in range(3):
                    project()
                down()
                down()
                start_normed()
                project()
                project()
                project()
                down()
                seen.settle(pe)
                with pe.Fori(0, (F_TILES - 2) // 2):
                    for _ in range(2):
                        project()
                        project()
                        down()
                    seen.settle(pe)
                down()
                seen.settle(pe)
            sums(square_sum, sum_ready)
            spread(spread_act)

        @block.scalar
        def _(act):
            seen = Seen()

            def prepare(m, g):
                act.wait_ge(h_new, seen(h_new))
                act.activation(x_hi[:, m, :], h[:, m, :], ACT.Copy, scale=g).then_inc(h_used, 1)
                act.activation(square_sum[:, :] if m == 0 else squares[m % 2][:, :], h[:, m, :], ACT.Square)\
                   .then_inc(h_used, 1)

            def keep_rstd():
                act.wait_ge(spread_act, seen(spread_act))
                act.activation(rstd_all[:, :], bank(SCORE, 2), ACT.Copy).then_inc(rstd_ready, 1)

            def keep_turned(out):
                act.wait_ge(turned_done, seen(turned_done))
                act.activation(out, ps[:, TURNED, 0:out.shape[-1]], ACT.Copy).then_inc(turned_out, 1)

            def keep_v():
                for g in range(2):
                    keep_turned(v_cur[:, 4 * g:4 * g + 4, :].rearrange("p b d -> p (b d)"))

            def keep_next():
                for new, cur in ((q_next, q_cur), (k_next, k_cur)):
                    act.wait_ge(next_ready, seen(next_ready))
                    act.activation(cur[:, :], new[:, :], ACT.Copy).then_inc(act_seq, 1)
                    act.wait_ge(act_seq, seen(act_seq))
                act.sem_inc(cur_ready, 1)
                act.sem_inc(next_free, 1)

            def attend(i, dilated):
                groups = [min(4, i + 1 - b) for _ in range(2 if dilated else 1) for b in range(0, i + 1, 4)]
                for n, blocks in enumerate(groups):
                    keep_turned(prob_t[:, n % 2, 0:blocks * P])
                act.wait_ge(turned_done, seen.count[turned_done]).then_inc(prob_free, 1)
                act.wait_ge(head_done, seen(head_done))
                act.activation(heads[:, i * P:(i + 1) * P], ps[:, HEAD, 0:P], ACT.Copy).then_inc(act_seq, 1)
                act.wait_ge(act_seq, seen(act_seq))
                act.sem_inc(head_free, 1)

            def exps(i, dilated):
                keys = (i + 1) * P
                act.wait_ge(top_ready, seen(top_ready))
                for j in range(2):
                    scores = prob[:, i % 2, j, 0:keys]
                    more = {} if dilated else {"accum_out": total[:, j:j + 1]}
                    act.activation(scores, scores, ACT.Exp, bias=neg_top[:, j:j + 1], scale=SCALE, **more)\
                       .then_inc(exp_done, 1)

            def keep_hi(source):
                act.wait_ge(value_ready, seen(value_ready))
                act.activation(mix_hi[:, :], source, ACT.Copy).then_inc(hi_ready, 1)

            def unit(dilated, next_attends=True):
                for i in range(QB):
                    if i:
                        attend(i - 1, dilated)
                    exps(i, dilated)
                attend(QB - 1, dilated)
                if dilated:
                    act.activation(mix_hi[:, :], heads[:, :], ACT.Copy).then_inc(hi_ready, 1)
                else:
                    act.activation(head_squares, heads[:, :], ACT.Square).then_inc(sq_ready, 1)
                if next_attends:
                    keep_next()
                    keep_v()
                if not dilated:
                    keep_hi(heads[:, :])

            def conv_center(out, tap):
                act.wait_ge(gate_ready, seen(gate_ready))
                act.activation(out, padded[:, TAPS - 1:], ACT.Copy, scale=tap).then_inc(gate_used, 1)

            def hidden(f):
                conv_center(k_next[:, :], taps[:, TAPS * (f % 2) + 2:TAPS * (f % 2) + 3])
                act.wait_ge(conv_ready, seen(conv_ready))
                act.activation(k_next[:, :], k_next[:, :], ACT.Silu).then_inc(silu_done, 1)
                keep_hi(k_next[:, :])

            act.sem_inc(head_free, 1)
            for m in range(KT):
                act.dma_start(h[:, m, :], x_t[m * P:(m + 1) * P, :]).then_inc(x_in[m], 16)
            act.dma_start(v_next[:, :].bitcast(i32), positions).then_inc(pos_in, 16)
            for m in range(KT):
                prepare(m, g0[:, m:m + 1])
            for wave, out in ((angle, sin_t), (turns, cos_t)):
                act.wait_ge(angle_ready, seen(angle_ready))
                act.activation(out[:, :], wave[:, :], ACT.Sin).then_inc(trig_done, 1)
            act.wait_ge(lam_summed, seen(lam_summed))
            act.activation(lam_exp[:, :], ps[:, TURNED, 0:2 * DEPTH], ACT.Exp).then_inc(lam_exped, 1)
            seen.settle(act)
            with act.Fori(0, DEPTH):
                keep_rstd()
                keep_next()
                keep_v()
                seen.settle(act)
                with act.Fori(0, A_UNITS):
                    unit(True)
                    seen.settle(act)
                with act.Fori(0, B_UNITS - 1):
                    unit(False)
                    seen.settle(act)
                unit(False, next_attends=False)
                for u, out in enumerate((k_next[:, :], k_cur[:, :])):
                    conv_center(out, lay[:, V_CONV_MIX + TAPS * u + 2:V_CONV_MIX + TAPS * u + 3])
                    keep_hi(heads[:, :])
                for m in range(KT):
                    prepare(m, lay[:, V_FFN_G + m:V_FFN_G + m + 1])
                keep_rstd()
                hidden(0)
                hidden(1)
                seen.settle(act)
                with act.Fori(0, (F_TILES - 2) // 2):
                    hidden(0)
                    hidden(1)
                    seen.settle(act)
                for m in range(KT):
                    prepare(m, lay[:, V_NEXT_G + m:V_NEXT_G + m + 1])
                seen.settle(act)
            keep_rstd()

        @block.vector
        def _(dve):
            seen = Seen()

            def evacuate(n, out):
                t = slice(n * HALF, (n + 1) * HALF)
                dve.wait_ge(half_done, seen(half_done))
                dve.tensor_tensor(out[:, t], bank(PROJ + n), rstd_all[:, t], ALU.mult).then_inc(dve_seq, 1)
                dve.wait_ge(dve_seq, seen(dve_seq))
                dve.sem_inc(half_free, 1)

            def absorb(m, g):
                dve.wait_ge(h_used, seen(h_used, 2))
                dve.scalar_tensor_tensor(x_lo[:, m, :], h[:, m, :], g, x_hi[:, m, :].bitcast(f32),
                                         ALU.mult, ALU.subtract).then_inc(dve_seq, 1)
                dve.wait_ge(dve_seq, seen(dve_seq))
                dve.sem_inc(x_ready, 1)
                if m:
                    dve.tensor_tensor(square_sum[:, :], square_sum[:, :], squares[m % 2][:, :], ALU.add).then_inc(dve_seq, 1)
                    dve.wait_ge(dve_seq, seen(dve_seq))
                if m == KT - 1:
                    dve.sem_inc(sum_ready, 1)

            def add_down(m):
                dve.wait_ge(down_done, seen(down_done))
                dve.tensor_tensor(h[:, m, :], bank(DOWN + 2 * (m % 2), 2), h[:, m, :], ALU.add).then_inc(dve_seq, 1)
                dve.wait_ge(dve_seq, seen(dve_seq))
                dve.sem_inc(down_free, 1)

            def add_last_down(g):
                for m in range(KT):
                    add_down(m)
                    dve.sem_inc(h_new, 1)
                    if m:
                        absorb(m - 1, lay[:, g + m - 1:g + m])
                absorb(KT - 1, lay[:, g + KT - 1:g + KT])

            def rsqrt_diagonal(width, eps, between=lambda: None):
                mean, y, t = rs[:, 0, :], rs[:, 1, :], rs[:, 2, :]
                dve.wait_ge(sum_done, seen(sum_done))
                dve.tensor_scalar(mean, ps[:, HEAD, 0:QB], 1.0 / width, eps, ALU.mult, ALU.add).then_inc(dve_seq, 1)
                dve.wait_ge(dve_seq, seen(dve_seq))
                dve.tensor_scalar(y.bitcast(i32), mean.bitcast(i32), 1, None, ALU.arith_shift_right).then_inc(dve_seq, 1)
                dve.wait_ge(dve_seq, seen(dve_seq))
                dve.tensor_scalar(y.bitcast(i32), y.bitcast(i32), -1.0, float(0x5F3759DF), ALU.mult, ALU.add).then_inc(dve_seq, 1)
                dve.wait_ge(dve_seq, seen(dve_seq))
                for _ in range(3):
                    dve.scalar_tensor_tensor(t, y, -0.5, y, ALU.mult, ALU.mult).then_inc(dve_seq, 1)
                    dve.wait_ge(dve_seq, seen(dve_seq))
                    dve.tensor_tensor(t, t, mean, ALU.mult).then_inc(dve_seq, 1)
                    dve.wait_ge(dve_seq, seen(dve_seq))
                    dve.scalar_tensor_tensor(y, t, 1.5, y, ALU.add, ALU.mult).then_inc(dve_seq, 1)
                    dve.wait_ge(dve_seq, seen(dve_seq))
                for b in range(QB):
                    dve.tensor_scalar(diagonal[:, b * P:(b + 1) * P], eye[:, :], y[:, b:b + 1], None, ALU.mult).then_inc(dve_seq, 1)
                    dve.wait_ge(dve_seq, seen(dve_seq))
                dve.sem_inc(diag_ready, 1)

            def start_norm():
                rsqrt_diagonal(D_MODEL, NORM_EPS)
                dve.wait_ge(rstd_ready, seen(rstd_ready))

            def rotate(x):
                swap = [p ^ (ROPE_DIMS // 2) for p in range(32)]
                dve.stream_shuffle(shuffled[:, :], x[:, :], swap).then_inc(dve_seq, 1)
                dve.wait_ge(dve_seq, seen(dve_seq))
                dve.tensor_tensor(shuffled[:, :], shuffled[:, :], sin_t[:, :], ALU.mult).then_inc(dve_seq, 1)
                dve.wait_ge(dve_seq, seen(dve_seq))
                dve.tensor_tensor(x[:, :], x[:, :], cos_t[:, :], ALU.mult).then_inc(dve_seq, 1)
                dve.wait_ge(dve_seq, seen(dve_seq))
                dve.tensor_tensor(x[:, :], x[:, :], shuffled[:, :], ALU.add).then_inc(dve_seq, 1)
                dve.wait_ge(dve_seq, seen(dve_seq))
                dve.sem_inc(next_ready, 1)

            def tops(i, dilated):
                keys = (i + 1) * P
                dve.wait_ge(score_done, seen(score_done))
                if i >= 2:
                    dve.wait_ge(prob_free, seen(prob_free))
                added = mask[:, 1 if dilated else 0, SEQ - keys:SEQ]
                for j in range(2):
                    dve.tensor_tensor_reduce(out=prob[:, i % 2, j, 0:keys], in0=bank(SCORE + 2 * j, 2)[:, 0:keys],
                                             in1=added, scale=1.0, scalar=-3e38, op0=ALU.add, op1=ALU.max,
                                             accum_out=top[:, j:j + 1]).then_inc(dve_seq, 1)
                    dve.wait_ge(dve_seq, seen(dve_seq))
                if i < QB - 1:
                    dve.sem_inc(score_free, 1)
                dve.tensor_scalar(neg_top[:, :], top[:, :], -SCALE, None, ALU.mult).then_inc(dve_seq, 1)
                dve.wait_ge(dve_seq, seen(dve_seq))
                dve.sem_inc(top_ready, 1)

            def normalise(i, dilated):
                keys = (i + 1) * P
                p0, p1 = prob[:, i % 2, 0, 0:keys], prob[:, i % 2, 1, 0:keys]
                dve.wait_ge(exp_done, seen(exp_done, 2))
                if dilated:
                    for j, p in enumerate((p0, p1)):
                        dve.tensor_tensor_reduce(out=p, in0=p, in1=mask[:, 2, SEQ - keys:SEQ], scale=1.0,
                                                 scalar=0.0, op0=ALU.mult, op1=ALU.add,
                                                 accum_out=total[:, j:j + 1]).then_inc(dve_seq, 1)
                        dve.wait_ge(dve_seq, seen(dve_seq))
                    dve.reciprocal(share[:, :], total[:, :]).then_inc(dve_seq, 1)
                    dve.wait_ge(dve_seq, seen(dve_seq))
                    for j, p in enumerate((p0, p1)):
                        dve.tensor_scalar(p, p, share[:, j:j + 1], None, ALU.mult).then_inc(dve_seq, 1)
                        dve.wait_ge(dve_seq, seen(dve_seq))
                else:
                    dve.reciprocal(share[:, :], total[:, :]).then_inc(dve_seq, 1)
                    dve.wait_ge(dve_seq, seen(dve_seq))
                    dve.tensor_scalar(p1, p1, share[:, 1:2], lay[:, V_NEG_LAM:V_NEG_LAM + 1], ALU.mult, ALU.mult).then_inc(dve_seq, 1)
                    dve.wait_ge(dve_seq, seen(dve_seq))
                    dve.scalar_tensor_tensor(p0, p0, share[:, 0:1], p1, ALU.mult, ALU.add).then_inc(dve_seq, 1)
                    dve.wait_ge(dve_seq, seen(dve_seq))
                dve.sem_inc(prob_ready, 1)

            def keep_lo(source):
                dve.wait_ge(hi_ready, seen(hi_ready))
                dve.tensor_tensor(mix_lo[:, :], source, mix_hi[:, :].bitcast(f32), ALU.subtract).then_inc(dve_seq, 1)
                dve.wait_ge(dve_seq, seen(dve_seq))
                dve.sem_inc(mix_ready, 1)

            def unit(dilated, next_attends=True):
                for i in range(QB):
                    tops(i, dilated)
                    if i == QB - 3 and next_attends:
                        dve.wait_ge(next_free, seen(next_free))
                    if i >= QB - 3:
                        n = i - (QB - 3)
                        evacuate(n % 2, (q_next, k_next)[n // 2])
                    normalise(i, dilated)
                evacuate(1, k_next)
                if next_attends:
                    rotate(q_next)
                dve.wait_ge(prob_free, seen(prob_free, 2))
                if dilated:
                    keep_lo(heads[:, :])
                else:
                    rsqrt_diagonal(P, SUBLN_EPS)
                evacuate(0, v_next)
                if next_attends:
                    rotate(k_next)
                evacuate(1, v_next)
                if next_attends:
                    dve.sem_inc(v_ready, 1)
                if not dilated:
                    dve.wait_ge(spread_dve, seen(spread_dve))
                    dve.scalar_tensor_tensor(heads[:, :], heads[:, :], lay[:, V_SUBLN_SCALED:V_SUBLN_SCALED + 1],
                                             bank(SCORE, 2), ALU.mult, ALU.mult).then_inc(dve_seq, 1)
                    dve.wait_ge(dve_seq, seen(dve_seq))
                    dve.sem_inc(value_ready, 1)
                    keep_lo(heads[:, :])
                for m in range(KT):
                    add_down(m)
                if next_attends:
                    dve.sem_inc(score_free, 1)

            def conv_taps(out, tap):
                dve.wait_ge(gate_used, seen(gate_used))
                for back in (1, 2):
                    dve.scalar_tensor_tensor(out[:, :], padded[:, TAPS - 1 - back:TAPS - 1 - back + SEQ],
                                             tap(TAPS - 1 - back), out[:, :], ALU.mult, ALU.add).then_inc(dve_seq, 1)
                    dve.wait_ge(dve_seq, seen(dve_seq))

            def hidden(f, down=True):
                for n in range(2):
                    evacuate(n, padded[:, TAPS - 1:])
                dve.sem_inc(gate_ready, 1)
                conv_taps(k_next, lambda j: taps[:, TAPS * (f % 2) + j:TAPS * (f % 2) + j + 1])
                dve.sem_inc(conv_ready, 1)
                for n in range(2):
                    evacuate(n, q_next)
                if down:
                    for m in range(KT):
                        add_down(m)
                dve.wait_ge(silu_done, seen(silu_done))
                dve.tensor_tensor(k_next[:, :], k_next[:, :], q_next[:, :], ALU.mult).then_inc(dve_seq, 1)
                dve.wait_ge(dve_seq, seen(dve_seq))
                dve.sem_inc(value_ready, 1)
                keep_lo(k_next[:, :])

            dve.memset(ones[:, :], 1.0).then_inc(dve_seq, 1)
            dve.wait_ge(dve_seq, seen(dve_seq))
            dve.memset(padded[:, 0:TAPS - 1], 0.0).then_inc(dve_seq, 1)
            dve.wait_ge(dve_seq, seen(dve_seq))
            dve.memset(neg_top[:, :], 0.0).then_inc(dve_seq, 1)
            dve.wait_ge(dve_seq, seen(dve_seq))
            dve.sem_inc(half_free, 2)
            dve.sem_inc(down_free, 2)
            dve.wait_ge(consts_in, seen(consts_in, 16 * 5))
            dve.sem_inc(w_free, 1)
            for m in range(KT):
                dve.wait_ge(x_in[m], seen(x_in[m], 16))
                dve.sem_inc(h_new, 1)
                if m:
                    absorb(m - 1, g0[:, m - 1:m])
            absorb(KT - 1, g0[:, KT - 1:KT])
            for layer in range(DEPTH):
                for n in range(2):
                    c = V_LAMBDA + 2 * n
                    dve.tensor_tensor(lam[:, 2 * layer + n:2 * layer + n + 1], vec[:, layer, c:c + 1],
                                      vec[:, layer, c + 1:c + 2], ALU.mult).then_inc(dve_seq, 1)
                    dve.wait_ge(dve_seq, seen(dve_seq))
            dve.sem_inc(consts_pe, 1)
            dve.wait_ge(pos_in, seen(pos_in, 16))
            dve.tensor_copy(angle[:, :], v_next[:, :].bitcast(i32)).then_inc(dve_seq, 1)
            dve.wait_ge(dve_seq, seen(dve_seq))
            dve.tensor_scalar(angle[:, :], angle[:, :], col[:, 0:1], None, ALU.mult).then_inc(dve_seq, 1)
            dve.wait_ge(dve_seq, seen(dve_seq))
            dve.tensor_scalar(turns[:, :], angle[:, :], 1 / TWO_PI, None, ALU.mult).then_inc(dve_seq, 1)
            dve.wait_ge(dve_seq, seen(dve_seq))
            dve.tensor_scalar(turns[:, :], turns[:, :], ROUNDER, None, ALU.add).then_inc(dve_seq, 1)
            dve.wait_ge(dve_seq, seen(dve_seq))
            dve.tensor_scalar(turns[:, :], turns[:, :], -ROUNDER, None, ALU.add).then_inc(dve_seq, 1)
            dve.wait_ge(dve_seq, seen(dve_seq))
            for part in (TURN_A, TURN_B, TURN_C):
                dve.scalar_tensor_tensor(angle[:, :], turns[:, :], -part, angle[:, :], ALU.mult, ALU.add).then_inc(dve_seq, 1)
                dve.wait_ge(dve_seq, seen(dve_seq))
            dve.tensor_scalar(angle[:, :], angle[:, :], -SIN_END, SIN_END, ALU.max, ALU.min).then_inc(dve_seq, 1)
            dve.wait_ge(dve_seq, seen(dve_seq))
            dve.sem_inc(angle_ready, 1)
            dve.tensor_scalar(turns[:, :], angle[:, :], -1.0, None, ALU.mult).then_inc(dve_seq, 1)
            dve.wait_ge(dve_seq, seen(dve_seq))
            dve.tensor_tensor(turns[:, :], turns[:, :], angle[:, :], ALU.min).then_inc(dve_seq, 1)
            dve.wait_ge(dve_seq, seen(dve_seq))
            dve.tensor_scalar(turns[:, :], turns[:, :], math.pi / 2, None, ALU.add).then_inc(dve_seq, 1)
            dve.wait_ge(dve_seq, seen(dve_seq))
            dve.sem_inc(angle_ready, 1)
            dve.wait_ge(trig_done, seen(trig_done, 2))
            dve.tensor_scalar(sin_t[:, :], sin_t[:, :], col[:, 1:2], None, ALU.mult).then_inc(dve_seq, 1)
            dve.wait_ge(dve_seq, seen(dve_seq))
            dve.wait_ge(lam_exped, seen(lam_exped))
            for layer in range(DEPTH):
                c = slice(V_NEG_LAM, V_NEG_LAM + 1)
                dve.tensor_tensor(vec[:, layer, c], lam_exp[:, 2 * layer + 1:2 * layer + 2],
                                  lam_exp[:, 2 * layer:2 * layer + 1], ALU.subtract).then_inc(dve_seq, 1)
                dve.wait_ge(dve_seq, seen(dve_seq))
                dve.tensor_tensor(vec[:, layer, c], vec[:, layer, c],
                                  vec[:, layer, V_LAM_INIT:V_LAM_INIT + 1], ALU.subtract).then_inc(dve_seq, 1)
                dve.wait_ge(dve_seq, seen(dve_seq))
                dve.tensor_tensor(vec[:, layer, V_SUBLN_SCALED:V_SUBLN_SCALED + 1],
                                  vec[:, layer, V_SUBLN:V_SUBLN + 1],
                                  vec[:, layer, V_ONE_LESS:V_ONE_LESS + 1], ALU.mult).then_inc(dve_seq, 1)
                dve.wait_ge(dve_seq, seen(dve_seq))
            seen.settle(dve)

            with dve.Fori(0, DEPTH) as layer:
                dve.tensor_copy(lay[:, :], vec[:, bass.ds(layer, 1), :].rearrange("p o v -> p (o v)")).then_inc(dve_seq, 1)
                dve.wait_ge(dve_seq, seen(dve_seq))
                start_norm()
                dve.sem_inc(score_free, 1)
                for out in (q_next, k_next):
                    for n in range(2):
                        evacuate(n, out)
                    rotate(out)
                for n in range(2):
                    evacuate(n, v_next)
                dve.sem_inc(v_ready, 1)
                seen.settle(dve)
                with dve.Fori(0, A_UNITS):
                    unit(True)
                    seen.settle(dve)
                with dve.Fori(0, B_UNITS - 1):
                    unit(False)
                    seen.settle(dve)
                dve.wait_ge(next_free, seen(next_free))
                unit(False, next_attends=False)

                v_flat = v_cur[:, :, :].rearrange("p b d -> p (b d)")
                second = (q_cur, k_cur, v_flat)

                def gate(c, x):
                    dve.tensor_tensor(padded[:, TAPS - 1:], c[:, :], x[:, :], ALU.mult).then_inc(dve_seq, 1)
                    dve.wait_ge(dve_seq, seen(dve_seq))
                    dve.sem_inc(gate_ready, 1)

                def convolve(u, b, c):
                    conv_taps(c, lambda j: lay[:, V_CONV_MIX + TAPS * u + j:V_CONV_MIX + TAPS * u + j + 1])
                    dve.tensor_tensor(heads[:, :], b[:, :], c[:, :], ALU.mult).then_inc(dve_seq, 1)
                    dve.wait_ge(dve_seq, seen(dve_seq))

                gate(k_next, v_next)
                evacuate(0, second[0])
                convolve(0, q_next, k_next)
                dve.sem_inc(value_ready, 1)
                evacuate(1, second[0])
                keep_lo(heads[:, :])
                for out in second[1:]:
                    for n in range(2):
                        evacuate(n, out)
                gate(second[1], second[2])
                convolve(1, second[0], second[1])
                for m in range(KT):
                    add_down(m)
                dve.sem_inc(value_ready, 1)
                keep_lo(heads[:, :])
                add_last_down(V_FFN_G)

                start_norm()

                def load_taps(at, n):
                    dve.tensor_copy(taps[:, 0:TAPS * n], lay[:, bass.ds(at, TAPS * n)]).then_inc(dve_seq, 1)
                    dve.wait_ge(dve_seq, seen(dve_seq))

                load_taps(V_CONV_FFN, 2)
                hidden(0, down=False)
                hidden(1)
                seen.settle(dve)
                with dve.Fori(1, F_TILES // 2) as pair:
                    load_taps(pair * (2 * TAPS) + V_CONV_FFN, 2)
                    hidden(0)
                    hidden(1)
                    seen.settle(dve)
                add_last_down(V_NEXT_G)
                seen.settle(dve)

            start_norm()
            for m in range(KT):
                dve.scalar_tensor_tensor(h[:, m, :], h[:, m, :], lay[:, V_NEXT_G + m:V_NEXT_G + m + 1],
                                         rstd_all[:, :], ALU.mult, ALU.mult).then_inc(dve_seq, 1)
                dve.wait_ge(dve_seq, seen(dve_seq))
                dve.sem_inc(out_ready, 1)



def by_feature(a):
    return np.reshape(a, (-1, P)).T


def weight_stream(w_in, w_out, w_up, w_down):
    def projection(w, c):
        return w[:, c:c + P].reshape(KT, P, P).transpose(1, 0, 2).reshape(P, KT * P)

    a_width, b_width, c_width = A_UNITS * P, B_UNITS * P, C_UNITS * P
    units = [[0 + u * P, a_width + u * P, 2 * a_width + u * P] for u in range(A_UNITS)]
    at = 3 * a_width
    units += [[at + u * P, at + b_width + u * P, at + 2 * b_width + u * P] for u in range(B_UNITS)]
    at += 3 * b_width
    units += [[at + u * P, at + c_width + u * P, at + 2 * c_width + u * P] for u in range(C_UNITS)]
    tiles = []
    for layer in range(DEPTH):
        tiles += [projection(w_in[layer], c) for c in units[0]]
        for u in range(MIX_UNITS):
            if u + 1 < MIX_UNITS:
                tiles += [projection(w_in[layer], c) for c in units[u + 1]]
            tiles.append(w_out[layer, u * P:(u + 1) * P])
        for f in range(F_TILES):
            tiles += [projection(w_up[layer], f * P), projection(w_up[layer], D_FF + f * P)]
            if f:
                tiles.append(w_down[layer, (f - 1) * P:f * P])
        tiles.append(w_down[layer, (F_TILES - 1) * P:])
    return np.stack(tiles)


def dilated_masks():
    d = np.arange(P)[:, None] + SEQ - P - np.arange(SEQ)[None, :]
    held = sum(((d >= 0) & (d % step == 0) & (d <= window)).astype(np.float32) for window, step in DILATED)
    return np.stack([np.where(d >= 0, 0.0, NEG), np.where(held > 0, 0.0, NEG), held], axis=1)


def kernel(x, positions, norm_mix_g, w_in, lambda_q1, lambda_k1, lambda_q2, lambda_k2, subln_g, conv_mix_w,
           w_out, norm_ffn_g, w_up, conv_ffn_w, w_down, final_g):
    import concourse.bacc as bacc
    from concourse.bass_utils import run_bass_kernel_spmd
    import ml_dtypes

    (x, positions, norm_mix_g, w_in, lambda_q1, lambda_k1, lambda_q2, lambda_k2, subln_g, conv_mix_w, w_out,
     norm_ffn_g, w_up, conv_ffn_w, w_down, final_g) = (
        np.asarray(a) for a in (x, positions, norm_mix_g, w_in, lambda_q1, lambda_k1, lambda_q2, lambda_k2,
                                subln_g, conv_mix_w, w_out, norm_ffn_g, w_up, conv_ffn_w, w_down, final_g))

    vectors = np.zeros((P, DEPTH, NV), np.float32)
    for layer in range(DEPTH):
        v = vectors[:, layer]
        v[:, V_FFN_G:V_FFN_G + KT] = by_feature(norm_ffn_g[layer])
        v[:, V_NEXT_G:V_NEXT_G + KT] = by_feature(norm_mix_g[layer + 1] if layer + 1 < DEPTH else final_g)
        for j in range(TAPS):
            v[:, V_CONV_MIX + j:V_CONV_FFN:TAPS] = by_feature(conv_mix_w[layer, j])
            v[:, V_CONV_FFN + j:V_SUBLN:TAPS] = by_feature(conv_ffn_w[layer, j])
        v[:, V_SUBLN] = subln_g[layer]
        for n, a in enumerate((lambda_q1, lambda_k1, lambda_q2, lambda_k2)):
            v[:HEAD_DIM, V_LAMBDA + n] = a[layer]
        lam_init = 0.8 - 0.6 * math.exp(-0.3 * layer)
        v[:, V_LAM_INIT], v[:, V_ONE_LESS] = lam_init, 1.0 - lam_init

    columns = np.zeros((P, 2), np.float32)
    half = ROPE_DIMS // 2
    freq = (np.float32(ROPE_THETA) ** (-(np.arange(half, dtype=np.float32) * np.float32(2.0) / ROPE_DIMS)))
    for start in (0, HEAD_DIM):
        columns[start:start + half] = np.stack([freq, -np.ones(half)], axis=1)
        columns[start + half:start + ROPE_DIMS] = np.stack([freq, np.ones(half)], axis=1)

    arrays = {
        "x_t": np.ascontiguousarray(x[0].T),
        "positions": np.ascontiguousarray(np.broadcast_to(positions, (P, SEQ))),
        "stream": weight_stream(w_in, w_out, w_up, w_down),
        "vectors": vectors.reshape(P, DEPTH * NV),
        "first_g": np.ascontiguousarray(by_feature(norm_mix_g[0])),
        "columns": columns,
        "square": np.eye(P, dtype=np.float32),
        "masks": dilated_masks().reshape(P, 3 * SEQ).astype(ml_dtypes.bfloat16),
    }
    nc = bacc.Bacc("TRN2", target_bir_lowering=False, num_devices=1)
    ins = [nc.dram_tensor(n, a.shape, mybir.dt.from_np(a.dtype), kind="ExternalInput").ap() for n, a in arrays.items()]
    out = nc.dram_tensor("out_t", (D_MODEL, SEQ), mybir.dt.float32, kind="ExternalOutput").ap()
    build(nc, *ins, out)
    result = run_bass_kernel_spmd(nc, [arrays], core_ids=[0])
    return np.ascontiguousarray(result.results[0]["out_t"].T)[None]
```

```python
import math
from contextlib import ExitStack

import numpy as np

import concourse.bass as bass
import concourse.mybir as mybir

P = 128
D_MODEL = 1024
SEQ = 1024
DEPTH = 2
HEAD_DIM = 64
A_UNITS = D_MODEL // 4 // P
B_UNITS = D_MODEL // 2 // P
C_UNITS = D_MODEL // 4 // P
D_FF = ((8 * D_MODEL // 3 + 127) // 128) * 128
F_TILES = D_FF // P
KT = D_MODEL // P
QB = SEQ // P
HALF = 512
TAPS = 3
DILATED = ((128, 1), (512, 4), (2048, 16))
ROPE_DIMS = HEAD_DIM // 4
ROPE_THETA = 500000.0
NORM_EPS, SUBLN_EPS = 1e-6, 1e-5
SCALE = HEAD_DIM ** -0.5
NEG = -1e30

MIX_UNITS = A_UNITS + B_UNITS + C_UNITS
LAYER_TILES = 4 * MIX_UNITS + 3 * F_TILES
TILES = DEPTH * LAYER_TILES
W_SLOTS = 2
DOWN_PAIRS = 3
FILLED = 4

V_FFN_G, V_NEXT_G = 0, KT
V_CONV_MIX = 2 * KT
V_CONV_FFN = V_CONV_MIX + TAPS * C_UNITS
V_SUBLN = V_CONV_FFN + TAPS * F_TILES
V_LAMBDA = V_SUBLN + 1
V_LAM_INIT = V_LAMBDA + 4
V_ONE_LESS = V_LAM_INIT + 1
V_NEG_LAM = V_ONE_LESS + 1
V_SUBLN_SCALED = V_NEG_LAM + 1
NV = V_SUBLN_SCALED + 1

TWO_PI = 2 * math.pi
TURN_A = 6.28125
TURN_B = float(np.float32(int((TWO_PI - TURN_A) * 2 ** 20) / 2 ** 20))
TURN_C = TWO_PI - TURN_A - TURN_B
ROUNDER = 1.5 * 2 ** 23
SIN_END = 3.1415925


class Seen:

    def __init__(self):
        self.count = {}

    def __call__(self, semaphore, n=1):
        self.count[semaphore] = self.count.get(semaphore, 0) + n
        return self.count[semaphore]

    def settle(self, engine):
        for semaphore, n in self.count.items():
            if n:
                engine.wait_ge(semaphore, n).then_inc(semaphore, -n)
                self.count[semaphore] = 0


def build(nc, x_t, positions, stream, vectors, first_g, columns, identity, masks, out_t):
    f32, f32r, bf16, i32 = (mybir.dt.float32, mybir.dt.float32r, mybir.dt.bfloat16, mybir.dt.int32)
    ALU, ACT = mybir.AluOpType, mybir.ActivationFunctionType
    ctx = ExitStack()
    with ctx:
        def sbuf(name, shape, dtype=f32):
            return ctx.enter_context(nc.sbuf_tensor(name, shape, dtype))

        def sem(name):
            return ctx.enter_context(nc.semaphore(name))

        h = sbuf("h", [P, KT, SEQ])
        x_hi = sbuf("x_hi", [P, KT, SEQ], f32r)
        x_lo = sbuf("x_lo", [P, KT, SEQ], f32r)
        stage = sbuf("stage", [P, W_SLOTS, D_MODEL])
        w_hi = sbuf("w_hi", [P, W_SLOTS, D_MODEL], f32r)
        w_lo = sbuf("w_lo", [P, W_SLOTS, D_MODEL], f32r)
        mix_hi = sbuf("mix_hi", [P, SEQ], f32r)
        mix_lo = sbuf("mix_lo", [P, SEQ], f32r)
        q_cur, k_cur = sbuf("q_cur", [P, SEQ]), sbuf("k_cur", [P, SEQ])
        v_cur = sbuf("v_cur", [P, QB, P])
        q_next, k_next = sbuf("q_next", [P, SEQ]), sbuf("k_next", [P, SEQ])
        v_next = sbuf("v_next", [P, SEQ])
        shuffled = sbuf("shuffled", [P, SEQ])
        prob = sbuf("prob", [P, 2, 2, SEQ])
        prob_t = sbuf("prob_t", [P, 2, HALF])
        heads = sbuf("heads", [P, QB, P])
        square = sbuf("square", [P, P])
        rstd_all = sbuf("rstd_all", [P, SEQ])
        padded = sbuf("padded", [P, TAPS - 1 + SEQ])
        cos_t, sin_t = sbuf("cos_t", [P, SEQ]), sbuf("sin_t", [P, SEQ])
        eye, ones = sbuf("eye", [P, P]), sbuf("ones", [P, P])
        mask = sbuf("mask", [P, 3, SEQ], bf16)
        vec = sbuf("vec", [P, DEPTH, NV])
        lay = sbuf("lay", [P, NV])
        g0 = sbuf("g0", [P, KT])
        col = sbuf("col", [P, 2])
        taps = sbuf("taps", [P, 2 * TAPS])
        lam = sbuf("lam", [P, 2 * DEPTH])
        lam_exp = sbuf("lam_exp", [P, 2 * DEPTH])
        neg_top = sbuf("neg_top", [P, 2, 2])
        total, share = sbuf("total", [P, 2, 2]), sbuf("share", [P, 2, 2])
        head_sums = sbuf("head_sums", [P, QB])
        rs = sbuf("rs", [P, 4, QB])
        ps = ctx.enter_context(nc.psum_tensor("ps", [P, 8, HALF], f32))

        turns, angle = q_next, k_next
        squares = (q_cur, k_cur)
        diagonal = prob[:, 0, 0, :]
        heads_flat = heads[:, :, :].rearrange("p b d -> p (b d)")

        def bank(b, n=1):
            return ps[:, b:b + n, :].rearrange("p b t -> p (b t)")

        PROJ, SCORE, TURNED, HEAD = 0, 2, 6, 7
        DOWN = SCORE

        stage_full = [sem(f"stage_full{s}") for s in range(W_SLOTS)]
        stage_free = sem("stage_free")
        w_ready, w_free = sem("w_ready"), sem("w_free")
        pool_seq = sem("pool_seq")
        consts_in, pos_in = sem("consts_in"), sem("pos_in")
        x_in = [sem(f"x_in{m}") for m in range(KT)]
        consts_pe = sem("consts_pe")
        dve_seq, act_seq = sem("dve_seq"), sem("act_seq")
        x_ready = sem("x_ready")
        half_done, half_free = sem("half_done"), sem("half_free")
        down_done, down_free = sem("down_done"), sem("down_free")
        mix_ready = sem("mix_ready")
        h_new, x_hi_ready = sem("h_new"), sem("x_hi_ready")
        squares_ready, squares_used = sem("squares_ready"), sem("squares_used")
        sum_done = sem("sum_done")
        diag_ready = sem("diag_ready")
        spread_done = sem("spread_done")
        rstd_ready = sem("rstd_ready")
        cur_ready = sem("cur_ready")
        next_ready, next_free = sem("next_ready"), sem("next_free")
        v_ready, v_turned = sem("v_ready"), sem("v_turned")
        v_kept = sem("v_kept")
        score_done, score_free = sem("score_done"), sem("score_free")
        top_ready, exp_done = sem("top_ready"), sem("exp_done")
        prob_ready, prob_free = sem("prob_ready"), sem("prob_free")
        turned_done, turned_out = sem("turned_done"), sem("turned_out")
        head_done, head_free = sem("head_done"), sem("head_free")
        head_sums_ready = sem("head_sums_ready")
        heads_ready = sem("heads_ready")
        heads_turned = sem("heads_turned")
        value_ready, hi_ready = sem("value_ready"), sem("hi_ready")
        gate_ready, gate_used = sem("gate_ready"), sem("gate_used")
        conv_ready, silu_done = sem("conv_ready"), sem("silu_done")
        angle_ready, trig_done = sem("angle_ready"), sem("trig_done")
        lam_summed = sem("lam_summed")
        lam_exped = sem("lam_exped")
        out_ready, out_done = sem("out_ready"), sem("out_done")

        block = ctx.enter_context(nc.Block())

        @block.sync
        def _(sp):
            seen = Seen()
            for source, tile in ((vectors, vec[:, :, :].rearrange("p l v -> p (l v)")), (first_g, g0[:, :]),
                                 (columns, col[:, :]), (identity, eye[:, :]),
                                 (masks, mask[:, :, :].rearrange("p m t -> p (m t)"))):
                sp.dma_start(tile, source).then_inc(consts_in, 16)
            rounds = stream.rearrange("(r s) p n -> r s p n", s=W_SLOTS)
            with sp.Fori(0, TILES // W_SLOTS) as r:
                for s in range(W_SLOTS):
                    sp.wait_ge(stage_free, seen(stage_free))
                    sp.dma_start(stage[:, s, :], rounds[bass.ds(r, 1), s, :, :].rearrange("o p n -> (o p) n"))\
                      .then_inc(stage_full[s], 16)
                seen.settle(sp)
            for m in range(KT):
                sp.wait_ge(out_ready, m + 1)
                sp.dma_start(out_t[m * P:(m + 1) * P, :], h[:, m, :]).then_inc(out_done, 16)
            sp.wait_ge(out_done, 16 * KT)

        @block.gpsimd
        def _(pool):
            seen = Seen()
            pool.sem_inc(stage_free, W_SLOTS)
            with pool.Fori(0, TILES // W_SLOTS):
                for s in range(W_SLOTS):
                    pool.wait_ge(stage_full[s], seen(stage_full[s], 16))
                    pool.wait_ge(w_free, seen(w_free))
                    pool.tensor_copy(w_hi[:, s, :], stage[:, s, :]).then_inc(pool_seq, 1)
                    pool.wait_ge(pool_seq, seen(pool_seq))
                    pool.tensor_tensor(w_lo[:, s, :], stage[:, s, :], w_hi[:, s, :].bitcast(f32), ALU.subtract)\
                        .then_inc(pool_seq, 1)
                    pool.wait_ge(pool_seq, seen(pool_seq))
                    pool.sem_inc(w_ready, 1)
                    pool.sem_inc(stage_free, 1)
                seen.settle(pool)

        @block.tensor
        def _(pe):
            seen = Seen()
            slot = [0]

            def next_slot():
                s = slot[0]
                slot[0] = (s + 1) % W_SLOTS
                return s

            def three_pass(out, slices, moving, start, stop):
                (s, w), (hi, lo) = slices, moving
                first = pe.matmul(out, w_hi[:, s, w], hi, start=start, stop=False)
                pe.matmul(out, w_hi[:, s, w], lo, start=False, stop=False)
                return first, pe.matmul(out, w_lo[:, s, w], hi, start=False, stop=stop)

            def project_half(s, n, first=False):
                t = slice(n * HALF, (n + 1) * HALF)
                if n == 0:
                    pe.wait_ge(w_ready, seen(w_ready))
                pe.wait_ge(half_free, seen(half_free))
                for k in range(KT):
                    if first and n == 0:
                        pe.wait_ge(x_ready, seen(x_ready))
                    begun, last = three_pass(bank(PROJ + n), (s, slice(k * P, (k + 1) * P)),
                                             (x_hi[:, k, t], x_lo[:, k, t]), k == 0, k == KT - 1)
                    if n == 0 and k == 0:
                        begun.then_inc(w_free, 1)
                last.then_inc(half_done, 1)

            def project(first=False):
                s = next_slot()
                for n in range(2):
                    project_half(s, n, first)

            def down(last=False):
                pairs = 2 if last else DOWN_PAIRS
                s = next_slot()
                pe.wait_ge(w_ready, seen(w_ready))
                pe.wait_ge(mix_ready, seen(mix_ready))
                for m in range(KT):
                    pe.wait_ge(down_free, seen(down_free))
                    for n in range(2):
                        t = slice(n * HALF, (n + 1) * HALF)
                        begun, ended = three_pass(bank(DOWN + 2 * (m % pairs) + n), (s, slice(m * P, (m + 1) * P)),
                                                  (mix_hi[:, t], mix_lo[:, t]), True, True)
                        if m == 0 and n == 0:
                            begun.then_inc(w_free, 1)
                    ended.then_inc(down_done, 1)
                    if last and m:
                        sum_squares(m - 1)
                if last:
                    sum_squares(KT - 1)

            def sum_squares(m):
                pe.wait_ge(squares_ready, seen(squares_ready))
                for b in range(QB):
                    last = pe.matmul(ps[:, HEAD, b:b + 1], squares[m % 2][:, b * P:(b + 1) * P], ones[:, 0:1],
                                     start=m == 0 and b == 0, stop=m == KT - 1, skip_group_check=True)
                if m == KT - 1:
                    last.then_inc(sum_done, 1)
                elif m < KT - 2:
                    last.then_inc(squares_used, 1)

            def start_normed():
                project(first=True)
                pe.wait_ge(diag_ready, seen(diag_ready))
                for n in range(2):
                    last = pe.matmul(bank(SCORE + n), ones[:, :], diagonal[:, n * HALF:(n + 1) * HALF],
                                     start=True, stop=True)
                last.then_inc(spread_done, 1)

            def scores(i, j):
                if i == 0 and j == 1:
                    pe.wait_ge(cur_ready, seen(cur_ready))
                pe.wait_ge(score_free, seen(score_free))
                keys = (i + 1) * P
                rows = slice(HEAD_DIM * j, HEAD_DIM * (j + 1))
                for n in range(0, keys, HALF):
                    wide = min(HALF, keys - n)
                    last = pe.matmul(ps[:, SCORE + 2 * j + n // HALF, 0:wide], q_cur[rows, i * P:(i + 1) * P],
                                     k_cur[rows, n:n + wide], start=True, stop=True)
                last.then_inc(score_done, 1)

            def turn(source, blocks):
                for b in range(blocks):
                    last = pe.transpose(ps[:, TURNED, b * P:(b + 1) * P], source[:, b * P:(b + 1) * P], eye[:, :])
                last.then_inc(turned_done, 1)

            def groups(i, dilated):
                return [(j, b, min(4, i + 1 - b)) for j in ((1, 0) if dilated else (0,)) for b in range(0, i + 1, 4)]

            def start_attend(i, dilated):
                j, b, blocks = groups(i, dilated)[0]
                pe.wait_ge(prob_ready, seen(prob_ready))
                turn(prob[:, i % 2, j, b * P:], blocks)

            def end_attend(i, dilated):
                todo = groups(i, dilated)
                pe.wait_ge(head_free, seen(head_free))
                for n, (j, b0, blocks) in enumerate(todo):
                    pe.wait_ge(turned_out, seen(turned_out))
                    if n + 1 < len(todo):
                        jn, bn, more = todo[n + 1]
                        if jn != j:
                            pe.wait_ge(prob_ready, seen(prob_ready))
                        turn(prob[:, i % 2, jn, bn * P:], more)
                    for b in range(b0, b0 + blocks):
                        dims = slice(HEAD_DIM * j, HEAD_DIM * (j + 1)) if dilated else slice(0, P)
                        last = pe.matmul(ps[:, HEAD, dims], prob_t[:, n % 2, (b - b0) * P:(b - b0 + 1) * P],
                                         v_cur[:, b, dims], start=b == 0, stop=b == i)
                last.then_inc(head_done, 1)

            def turn_v():
                pe.wait_ge(v_ready, seen(v_ready))
                for b in range(QB):
                    last = pe.transpose(ps[:, TURNED + b // 4, (b % 4) * P:(b % 4 + 1) * P],
                                        v_next[:, b * P:(b + 1) * P], eye[:, :])
                last.then_inc(v_turned, 1)

            def turn_heads():
                pe.wait_ge(heads_ready, seen(heads_ready))
                for b in range(QB):
                    last = pe.transpose(ps[:, SCORE + b // 4, (b % 4) * P:(b % 4 + 1) * P], heads[:, b, :], eye[:, :])
                last.then_inc(heads_turned, 1)

            def unit(dilated):
                for i in range(QB):
                    if i < FILLED:
                        s = s if i % 2 else next_slot()
                        project_half(s, i % 2)
                    if i == 0:
                        turn_v()
                    scores(i, 1)
                    if i:
                        start_attend(i - 1, dilated)
                    scores(i, 0)
                    if i == 1:
                        pe.wait_ge(v_kept, seen(v_kept))
                    if i:
                        end_attend(i - 1, dilated)
                start_attend(QB - 1, dilated)
                end_attend(QB - 1, dilated)
                s = next_slot()
                project_half(s, 0)
                turn_heads()
                project_half(s, 1)
                down()

            pe.wait_ge(consts_pe, seen(consts_pe))
            pe.matmul(ps[:, TURNED, 0:2 * DEPTH], ones[:, :], lam[:, :], start=True, stop=True).then_inc(lam_summed, 1)
            for m in range(KT):
                sum_squares(m)
            seen.settle(pe)
            with pe.Fori(0, DEPTH):
                start_normed()
                project()
                project()
                seen.settle(pe)
                with pe.Fori(0, A_UNITS):
                    unit(True)
                    seen.settle(pe)
                with pe.Fori(0, B_UNITS - 1):
                    unit(False)
                    seen.settle(pe)
                unit(False)
                for _ in range(3):
                    project()
                down()
                down(last=True)
                start_normed()
                project()
                project()
                project()
                down()
                seen.settle(pe)
                with pe.Fori(0, (F_TILES - 2) // 2):
                    for _ in range(2):
                        project()
                        project()
                        down()
                    seen.settle(pe)
                down(last=True)
                seen.settle(pe)
            pe.wait_ge(diag_ready, seen(diag_ready))
            for n in range(2):
                last = pe.matmul(bank(SCORE + n), ones[:, :], diagonal[:, n * HALF:(n + 1) * HALF],
                                 start=True, stop=True)
            last.then_inc(spread_done, 1)

        @block.scalar
        def _(act):
            seen = Seen()

            def prepare(m, g):
                act.wait_ge(h_new, seen(h_new))
                act.activation(x_hi[:, m, :], h[:, m, :], ACT.Copy, scale=g).then_inc(x_hi_ready, 1)
                if m >= 2:
                    act.wait_ge(squares_used, seen(squares_used))
                act.activation(squares[m % 2][:, :], h[:, m, :], ACT.Square).then_inc(squares_ready, 1)

            def keep_rstd():
                act.wait_ge(spread_done, seen(spread_done))
                act.activation(rstd_all[:, :], bank(SCORE, 2), ACT.Copy).then_inc(rstd_ready, 1)

            def keep_turned(out):
                act.wait_ge(turned_done, seen(turned_done))
                act.activation(out, ps[:, TURNED, 0:out.shape[-1]], ACT.Copy).then_inc(turned_out, 1)

            def keep_v():
                act.wait_ge(v_turned, seen(v_turned))
                act.activation(v_cur[:, :, :].rearrange("p b d -> p (b d)"), bank(TURNED, 2), ACT.Copy)\
                   .then_inc(v_kept, 1)

            def keep_next():
                for new, cur in ((q_next, q_cur), (k_next, k_cur)):
                    act.wait_ge(next_ready, seen(next_ready))
                    act.activation(cur[:, :], new[:, :], ACT.Copy).then_inc(act_seq, 1)
                    act.wait_ge(act_seq, seen(act_seq))
                act.sem_inc(cur_ready, 1)
                act.sem_inc(next_free, 1)

            def keep_head(i, dilated):
                act.wait_ge(head_done, seen(head_done))
                if dilated:
                    for j in range(2):
                        dims = slice(HEAD_DIM * j, HEAD_DIM * (j + 1))
                        act.activation(heads[:, i, dims], ps[:, HEAD, dims], ACT.Copy, scale=share[:, i % 2, j:j + 1])\
                           .then_inc(act_seq, 1)
                        act.wait_ge(act_seq, seen(act_seq))
                else:
                    act.activation(heads[:, i, :], ps[:, HEAD, 0:P], ACT.Copy).then_inc(act_seq, 1)
                    act.wait_ge(act_seq, seen(act_seq))
                    act.activation(square[:, :], ps[:, HEAD, 0:P], ACT.Square, accum_out=head_sums[:, i:i + 1])\
                       .then_inc(act_seq, 1)
                    act.wait_ge(act_seq, seen(act_seq))
                act.sem_inc(head_free, 1)

            def exps(i, j, dilated):
                scores = prob[:, i % 2, j, 0:(i + 1) * P]
                more = {} if dilated else {"accum_out": total[:, i % 2, j:j + 1]}
                act.wait_ge(top_ready, seen(top_ready))
                act.activation(scores, scores, ACT.Exp, bias=neg_top[:, i % 2, j:j + 1], scale=-1.0, **more)\
                   .then_inc(exp_done, 1)

            def keep_hi(source):
                act.wait_ge(value_ready, seen(value_ready))
                act.activation(mix_hi[:, :], source, ACT.Copy).then_inc(hi_ready, 1)

            def unit(dilated, next_attends=True):
                keep_v()
                exps(0, 1, dilated)
                exps(0, 0, dilated)
                for i in range(QB):
                    sizes = [min(4, i + 1 - b) for _ in range(2 if dilated else 1) for b in range(0, i + 1, 4)]
                    for n in range(max(2, len(sizes))):
                        if n < len(sizes):
                            keep_turned(prob_t[:, n % 2, 0:sizes[n] * P])
                        if n < 2 and i + 1 < QB:
                            exps(i + 1, 1 - n, dilated)
                    act.wait_ge(turned_done, seen.count[turned_done]).then_inc(prob_free, 1)
                    keep_head(i, dilated)
                act.sem_inc(heads_ready if dilated else head_sums_ready, 1)
                if next_attends:
                    keep_next()
                act.wait_ge(heads_turned, seen(heads_turned))
                gain = 1.0 if dilated else lay[:, V_SUBLN_SCALED:V_SUBLN_SCALED + 1]
                act.activation(mix_hi[:, :], bank(SCORE, 2), ACT.Copy, scale=gain).then_inc(hi_ready, 1)

            def conv_center(out, tap):
                act.wait_ge(gate_ready, seen(gate_ready))
                act.activation(out, padded[:, TAPS - 1:], ACT.Copy, scale=tap).then_inc(gate_used, 1)

            def hidden(f):
                conv_center(k_next[:, :], taps[:, TAPS * (f % 2) + 2:TAPS * (f % 2) + 3])
                act.wait_ge(conv_ready, seen(conv_ready))
                act.activation(k_next[:, :], k_next[:, :], ACT.Silu).then_inc(silu_done, 1)
                keep_hi(k_next[:, :])

            act.sem_inc(head_free, 1)
            act.dma_start(v_next[:, :].bitcast(i32), positions).then_inc(pos_in, 16)
            for m in range(KT):
                act.dma_start(h[:, m, :], x_t[m * P:(m + 1) * P, :]).then_inc(x_in[m], 16)
            for m in range(KT):
                prepare(m, g0[:, m:m + 1])
            for wave, out in ((angle, sin_t), (turns, cos_t)):
                act.wait_ge(angle_ready, seen(angle_ready))
                act.activation(out[:, :], wave[:, :], ACT.Sin).then_inc(trig_done, 1)
            act.wait_ge(lam_summed, seen(lam_summed))
            act.activation(lam_exp[:, :], ps[:, TURNED, 0:2 * DEPTH], ACT.Exp).then_inc(lam_exped, 1)
            seen.settle(act)
            with act.Fori(0, DEPTH):
                keep_rstd()
                keep_next()
                seen.settle(act)
                with act.Fori(0, A_UNITS):
                    unit(True)
                    seen.settle(act)
                with act.Fori(0, B_UNITS - 1):
                    unit(False)
                    seen.settle(act)
                unit(False, next_attends=False)
                for u, out in enumerate((k_next[:, :], k_cur[:, :])):
                    conv_center(out, lay[:, V_CONV_MIX + TAPS * u + 2:V_CONV_MIX + TAPS * u + 3])
                    keep_hi(heads_flat)
                for m in range(KT):
                    prepare(m, lay[:, V_FFN_G + m:V_FFN_G + m + 1])
                keep_rstd()
                hidden(0)
                hidden(1)
                seen.settle(act)
                with act.Fori(0, (F_TILES - 2) // 2):
                    hidden(0)
                    hidden(1)
                    seen.settle(act)
                for m in range(KT):
                    prepare(m, lay[:, V_NEXT_G + m:V_NEXT_G + m + 1])
                seen.settle(act)
            keep_rstd()

        @block.vector
        def _(dve):
            seen = Seen()

            def evacuate(n, out):
                t = slice(n * HALF, (n + 1) * HALF)
                dve.wait_ge(half_done, seen(half_done))
                dve.tensor_tensor(out[:, t], bank(PROJ + n), rstd_all[:, t], ALU.mult).then_inc(dve_seq, 1)
                dve.wait_ge(dve_seq, seen(dve_seq))
                dve.sem_inc(half_free, 1)

            def absorb(m, g):
                dve.wait_ge(x_hi_ready, seen(x_hi_ready))
                dve.scalar_tensor_tensor(x_lo[:, m, :], h[:, m, :], g, x_hi[:, m, :].bitcast(f32),
                                         ALU.mult, ALU.subtract).then_inc(dve_seq, 1)
                dve.wait_ge(dve_seq, seen(dve_seq))
                dve.sem_inc(x_ready, 1)

            def add_down(m, pairs=DOWN_PAIRS):
                dve.wait_ge(down_done, seen(down_done))
                dve.tensor_tensor(h[:, m, :], bank(DOWN + 2 * (m % pairs), 2), h[:, m, :], ALU.add)\
                   .then_inc(dve_seq, 1)
                dve.wait_ge(dve_seq, seen(dve_seq))
                dve.sem_inc(down_free, 1)

            def add_last_down(g):
                for m in range(KT):
                    add_down(m, 2)
                    dve.sem_inc(h_new, 1)
                    if m:
                        absorb(m - 1, lay[:, g + m - 1:g + m])
                absorb(KT - 1, lay[:, g + KT - 1:g + KT])

            def rsqrt(sums, width, eps):
                mean, y, t = rs[:, 0, :], rs[:, 1, :], rs[:, 2, :]
                dve.tensor_scalar(mean, sums, 1.0 / width, eps, ALU.mult, ALU.add).then_inc(dve_seq, 1)
                dve.wait_ge(dve_seq, seen(dve_seq))
                dve.tensor_scalar(y.bitcast(i32), mean.bitcast(i32), 1, None, ALU.arith_shift_right)\
                   .then_inc(dve_seq, 1)
                dve.wait_ge(dve_seq, seen(dve_seq))
                dve.tensor_scalar(y.bitcast(i32), y.bitcast(i32), -1.0, float(0x5F3759DF), ALU.mult, ALU.add)\
                   .then_inc(dve_seq, 1)
                dve.wait_ge(dve_seq, seen(dve_seq))
                for _ in range(3):
                    dve.scalar_tensor_tensor(t, y, -0.5, y, ALU.mult, ALU.mult).then_inc(dve_seq, 1)
                    dve.wait_ge(dve_seq, seen(dve_seq))
                    dve.tensor_tensor(t, t, mean, ALU.mult).then_inc(dve_seq, 1)
                    dve.wait_ge(dve_seq, seen(dve_seq))
                    dve.scalar_tensor_tensor(y, t, 1.5, y, ALU.add, ALU.mult).then_inc(dve_seq, 1)
                    dve.wait_ge(dve_seq, seen(dve_seq))
                return y

            def start_norm():
                dve.wait_ge(sum_done, seen(sum_done))
                y = rsqrt(ps[:, HEAD, 0:QB], D_MODEL, NORM_EPS)
                for b in range(QB):
                    dve.tensor_scalar(diagonal[:, b * P:(b + 1) * P], eye[:, :], y[:, b:b + 1], None, ALU.mult)\
                       .then_inc(dve_seq, 1)
                dve.wait_ge(dve_seq, seen(dve_seq, QB))
                dve.sem_inc(diag_ready, 1)
                dve.wait_ge(rstd_ready, seen(rstd_ready))

            def rotate(x):
                swap = [p ^ (ROPE_DIMS // 2) for p in range(32)]
                dve.stream_shuffle(shuffled[:, :], x[:, :], swap).then_inc(dve_seq, 1)
                dve.wait_ge(dve_seq, seen(dve_seq))
                dve.tensor_tensor(shuffled[:, :], shuffled[:, :], sin_t[:, :], ALU.mult).then_inc(dve_seq, 1)
                dve.wait_ge(dve_seq, seen(dve_seq))
                dve.tensor_tensor(x[:, :], x[:, :], cos_t[:, :], ALU.mult).then_inc(dve_seq, 1)
                dve.wait_ge(dve_seq, seen(dve_seq))
                dve.tensor_tensor(x[:, :], x[:, :], shuffled[:, :], ALU.add).then_inc(dve_seq, 1)
                dve.wait_ge(dve_seq, seen(dve_seq))
                dve.sem_inc(next_ready, 1)

            def tops(i, dilated):
                keys, at = (i + 1) * P, i % 2
                if i >= 2:
                    dve.wait_ge(prob_free, seen(prob_free))
                for j in (1, 0):
                    dve.wait_ge(score_done, seen(score_done))
                    dve.tensor_tensor_reduce(out=prob[:, at, j, 0:keys], in0=bank(SCORE + 2 * j, 2)[:, 0:keys],
                                             in1=mask[:, 1 if dilated else 0, SEQ - keys:SEQ], scale=-SCALE,
                                             scalar=3e38, op0=ALU.add, op1=ALU.min,
                                             accum_out=neg_top[:, at, j:j + 1]).then_inc(dve_seq, 1)
                    dve.wait_ge(dve_seq, seen(dve_seq))
                    dve.sem_inc(top_ready, 1)
                    if i < QB - 1:
                        dve.sem_inc(score_free, 1)

            def weigh(i):
                keys, at = (i + 1) * P, i % 2
                for j in (1, 0):
                    dve.wait_ge(exp_done, seen(exp_done))
                    dve.tensor_tensor_reduce(out=prob[:, at, j, 0:keys], in0=prob[:, at, j, 0:keys],
                                             in1=mask[:, 2, SEQ - keys:SEQ], scale=1.0, scalar=0.0,
                                             op0=ALU.mult, op1=ALU.add, accum_out=total[:, at, j:j + 1])\
                       .then_inc(dve_seq, 1)
                    dve.wait_ge(dve_seq, seen(dve_seq))
                    if j == 0:
                        dve.reciprocal(share[:, at, :], total[:, at, :]).then_inc(dve_seq, 1)
                        dve.wait_ge(dve_seq, seen(dve_seq))
                    dve.sem_inc(prob_ready, 1)

            def subtract(i):
                keys, at = (i + 1) * P, i % 2
                p0, p1 = prob[:, at, 0, 0:keys], prob[:, at, 1, 0:keys]
                dve.wait_ge(exp_done, seen(exp_done))
                dve.reciprocal(share[:, at, 1:2], total[:, at, 1:2]).then_inc(dve_seq, 1)
                dve.wait_ge(dve_seq, seen(dve_seq))
                dve.tensor_scalar(p1, p1, share[:, at, 1:2], lay[:, V_NEG_LAM:V_NEG_LAM + 1], ALU.mult, ALU.mult)\
                   .then_inc(dve_seq, 1)
                dve.wait_ge(exp_done, seen(exp_done))
                dve.reciprocal(share[:, at, 0:1], total[:, at, 0:1]).then_inc(dve_seq, 1)
                dve.wait_ge(dve_seq, seen(dve_seq, 2))
                dve.scalar_tensor_tensor(p0, p0, share[:, at, 0:1], p1, ALU.mult, ALU.add).then_inc(dve_seq, 1)
                dve.wait_ge(dve_seq, seen(dve_seq))
                dve.sem_inc(prob_ready, 1)

            def keep_lo(source, gain=1.0):
                dve.wait_ge(hi_ready, seen(hi_ready))
                dve.scalar_tensor_tensor(mix_lo[:, :], source, gain, mix_hi[:, :].bitcast(f32),
                                         ALU.mult, ALU.subtract).then_inc(dve_seq, 1)
                dve.wait_ge(dve_seq, seen(dve_seq))
                dve.sem_inc(mix_ready, 1)

            def unit(dilated, next_attends=True):
                halves = [(x, n) for x in (q_next, k_next) for n in range(2)]
                dve.wait_ge(next_free, seen(next_free))
                for i in range(QB):
                    if i < FILLED:
                        x, n = halves[i]
                        evacuate(n, x)
                    tops(i, dilated)
                    if i == 1 and next_attends:
                        rotate(q_next)
                    weigh(i) if dilated else subtract(i)
                if next_attends:
                    rotate(k_next)
                dve.wait_ge(prob_free, seen(prob_free, 2))
                if not dilated:
                    dve.wait_ge(head_sums_ready, seen(head_sums_ready))
                    y = rsqrt(head_sums[:, :], P, SUBLN_EPS)
                    for b in range(QB):
                        dve.tensor_scalar(heads[:, b, :], heads[:, b, :], y[:, b:b + 1], None, ALU.mult)\
                           .then_inc(dve_seq, 1)
                    dve.wait_ge(dve_seq, seen(dve_seq, QB))
                    dve.sem_inc(heads_ready, 1)
                evacuate(0, v_next)
                if dilated:
                    keep_lo(bank(SCORE, 2))
                else:
                    keep_lo(bank(SCORE, 2), lay[:, V_SUBLN_SCALED:V_SUBLN_SCALED + 1])
                evacuate(1, v_next)
                for m in range(KT):
                    add_down(m)
                if next_attends:
                    dve.sem_inc(v_ready, 1)
                    dve.sem_inc(score_free, 2)

            def conv_taps(out, tap):
                dve.wait_ge(gate_used, seen(gate_used))
                for back in (1, 2):
                    dve.scalar_tensor_tensor(out[:, :], padded[:, TAPS - 1 - back:TAPS - 1 - back + SEQ],
                                             tap(TAPS - 1 - back), out[:, :], ALU.mult, ALU.add).then_inc(dve_seq, 1)
                    dve.wait_ge(dve_seq, seen(dve_seq))

            def hidden(f, down=True):
                for n in range(2):
                    evacuate(n, padded[:, TAPS - 1:])
                dve.sem_inc(gate_ready, 1)
                conv_taps(k_next, lambda j: taps[:, TAPS * (f % 2) + j:TAPS * (f % 2) + j + 1])
                dve.sem_inc(conv_ready, 1)
                for n in range(2):
                    evacuate(n, q_next)
                if down:
                    for m in range(KT):
                        add_down(m)
                dve.wait_ge(silu_done, seen(silu_done))
                dve.tensor_tensor(k_next[:, :], k_next[:, :], q_next[:, :], ALU.mult).then_inc(dve_seq, 1)
                dve.wait_ge(dve_seq, seen(dve_seq))
                dve.sem_inc(value_ready, 1)
                keep_lo(k_next[:, :])

            dve.memset(ones[:, :], 1.0).then_inc(dve_seq, 1)
            dve.wait_ge(dve_seq, seen(dve_seq))
            dve.memset(padded[:, 0:TAPS - 1], 0.0).then_inc(dve_seq, 1)
            dve.wait_ge(dve_seq, seen(dve_seq))
            dve.sem_inc(half_free, 2)
            dve.sem_inc(down_free, DOWN_PAIRS)
            dve.sem_inc(w_free, 1)
            dve.wait_ge(consts_in, seen(consts_in, 16 * 5))
            for layer in range(DEPTH):
                for n in range(2):
                    c = V_LAMBDA + 2 * n
                    dve.tensor_tensor(lam[:, 2 * layer + n:2 * layer + n + 1], vec[:, layer, c:c + 1],
                                      vec[:, layer, c + 1:c + 2], ALU.mult).then_inc(dve_seq, 1)
                    dve.wait_ge(dve_seq, seen(dve_seq))
            dve.sem_inc(consts_pe, 1)
            dve.wait_ge(pos_in, seen(pos_in, 16))
            dve.tensor_copy(angle[:, :], v_next[:, :].bitcast(i32)).then_inc(dve_seq, 1)
            dve.wait_ge(dve_seq, seen(dve_seq))
            dve.tensor_scalar(angle[:, :], angle[:, :], col[:, 0:1], None, ALU.mult).then_inc(dve_seq, 1)
            dve.wait_ge(dve_seq, seen(dve_seq))
            dve.tensor_scalar(turns[:, :], angle[:, :], 1 / TWO_PI, None, ALU.mult).then_inc(dve_seq, 1)
            dve.wait_ge(dve_seq, seen(dve_seq))
            dve.tensor_scalar(turns[:, :], turns[:, :], ROUNDER, None, ALU.add).then_inc(dve_seq, 1)
            dve.wait_ge(dve_seq, seen(dve_seq))
            dve.tensor_scalar(turns[:, :], turns[:, :], -ROUNDER, None, ALU.add).then_inc(dve_seq, 1)
            dve.wait_ge(dve_seq, seen(dve_seq))
            for part in (TURN_A, TURN_B, TURN_C):
                dve.scalar_tensor_tensor(angle[:, :], turns[:, :], -part, angle[:, :], ALU.mult, ALU.add).then_inc(dve_seq, 1)
                dve.wait_ge(dve_seq, seen(dve_seq))
            dve.tensor_scalar(angle[:, :], angle[:, :], -SIN_END, SIN_END, ALU.max, ALU.min).then_inc(dve_seq, 1)
            dve.wait_ge(dve_seq, seen(dve_seq))
            dve.sem_inc(angle_ready, 1)
            dve.tensor_scalar(turns[:, :], angle[:, :], -1.0, None, ALU.mult).then_inc(dve_seq, 1)
            dve.wait_ge(dve_seq, seen(dve_seq))
            dve.tensor_tensor(turns[:, :], turns[:, :], angle[:, :], ALU.min).then_inc(dve_seq, 1)
            dve.wait_ge(dve_seq, seen(dve_seq))
            dve.tensor_scalar(turns[:, :], turns[:, :], math.pi / 2, None, ALU.add).then_inc(dve_seq, 1)
            dve.wait_ge(dve_seq, seen(dve_seq))
            dve.sem_inc(angle_ready, 1)
            for m in range(KT):
                dve.wait_ge(x_in[m], seen(x_in[m], 16))
                dve.sem_inc(h_new, 1)
                if m:
                    absorb(m - 1, g0[:, m - 1:m])
            absorb(KT - 1, g0[:, KT - 1:KT])
            dve.wait_ge(trig_done, seen(trig_done, 2))
            dve.tensor_scalar(sin_t[:, :], sin_t[:, :], col[:, 1:2], None, ALU.mult).then_inc(dve_seq, 1)
            dve.wait_ge(dve_seq, seen(dve_seq))
            dve.wait_ge(lam_exped, seen(lam_exped))
            for layer in range(DEPTH):
                c = slice(V_NEG_LAM, V_NEG_LAM + 1)
                dve.tensor_tensor(vec[:, layer, c], lam_exp[:, 2 * layer + 1:2 * layer + 2],
                                  lam_exp[:, 2 * layer:2 * layer + 1], ALU.subtract).then_inc(dve_seq, 1)
                dve.wait_ge(dve_seq, seen(dve_seq))
                dve.tensor_tensor(vec[:, layer, c], vec[:, layer, c],
                                  vec[:, layer, V_LAM_INIT:V_LAM_INIT + 1], ALU.subtract).then_inc(dve_seq, 1)
                dve.wait_ge(dve_seq, seen(dve_seq))
                dve.tensor_tensor(vec[:, layer, V_SUBLN_SCALED:V_SUBLN_SCALED + 1],
                                  vec[:, layer, V_SUBLN:V_SUBLN + 1],
                                  vec[:, layer, V_ONE_LESS:V_ONE_LESS + 1], ALU.mult).then_inc(dve_seq, 1)
                dve.wait_ge(dve_seq, seen(dve_seq))
            seen.settle(dve)

            with dve.Fori(0, DEPTH) as layer:
                dve.tensor_copy(lay[:, :], vec[:, bass.ds(layer, 1), :].rearrange("p o v -> p (o v)")).then_inc(dve_seq, 1)
                dve.wait_ge(dve_seq, seen(dve_seq))
                start_norm()
                dve.sem_inc(score_free, 2)
                for out in (q_next, k_next):
                    for n in range(2):
                        evacuate(n, out)
                    rotate(out)
                for n in range(2):
                    evacuate(n, v_next)
                dve.sem_inc(v_ready, 1)
                seen.settle(dve)
                with dve.Fori(0, A_UNITS):
                    unit(True)
                    seen.settle(dve)
                with dve.Fori(0, B_UNITS - 1):
                    unit(False)
                    seen.settle(dve)
                unit(False, next_attends=False)

                v_flat = v_cur[:, :, :].rearrange("p b d -> p (b d)")
                second = (q_cur, k_cur, v_flat)

                def gate(c, x):
                    dve.tensor_tensor(padded[:, TAPS - 1:], c[:, :], x[:, :], ALU.mult).then_inc(dve_seq, 1)
                    dve.wait_ge(dve_seq, seen(dve_seq))
                    dve.sem_inc(gate_ready, 1)

                def convolve(u, b, c):
                    conv_taps(c, lambda j: lay[:, V_CONV_MIX + TAPS * u + j:V_CONV_MIX + TAPS * u + j + 1])
                    dve.tensor_tensor(heads_flat, b[:, :], c[:, :], ALU.mult).then_inc(dve_seq, 1)
                    dve.wait_ge(dve_seq, seen(dve_seq))

                gate(k_next, v_next)
                evacuate(0, second[0])
                convolve(0, q_next, k_next)
                dve.sem_inc(value_ready, 1)
                evacuate(1, second[0])
                keep_lo(heads_flat)
                for out in second[1:]:
                    for n in range(2):
                        evacuate(n, out)
                gate(second[1], second[2])
                convolve(1, second[0], second[1])
                for m in range(KT):
                    add_down(m)
                dve.sem_inc(value_ready, 1)
                keep_lo(heads_flat)
                add_last_down(V_FFN_G)

                start_norm()

                def load_taps(at, n):
                    dve.tensor_copy(taps[:, 0:TAPS * n], lay[:, bass.ds(at, TAPS * n)]).then_inc(dve_seq, 1)
                    dve.wait_ge(dve_seq, seen(dve_seq))

                load_taps(V_CONV_FFN, 2)
                hidden(0, down=False)
                hidden(1)
                seen.settle(dve)
                with dve.Fori(1, F_TILES // 2) as pair:
                    load_taps(pair * (2 * TAPS) + V_CONV_FFN, 2)
                    hidden(0)
                    hidden(1)
                    seen.settle(dve)
                add_last_down(V_NEXT_G)
                seen.settle(dve)

            start_norm()
            for m in range(KT):
                dve.scalar_tensor_tensor(h[:, m, :], h[:, m, :], lay[:, V_NEXT_G + m:V_NEXT_G + m + 1],
                                         rstd_all[:, :], ALU.mult, ALU.mult).then_inc(dve_seq, 1)
                dve.wait_ge(dve_seq, seen(dve_seq))
                dve.sem_inc(out_ready, 1)



def by_feature(a):
    return np.reshape(a, (-1, P)).T


def weight_stream(w_in, w_out, w_up, w_down):
    def projection(w, c):
        return w[:, c:c + P].reshape(KT, P, P).transpose(1, 0, 2).reshape(P, KT * P)

    a_width, b_width, c_width = A_UNITS * P, B_UNITS * P, C_UNITS * P
    units = [[0 + u * P, a_width + u * P, 2 * a_width + u * P] for u in range(A_UNITS)]
    at = 3 * a_width
    units += [[at + u * P, at + b_width + u * P, at + 2 * b_width + u * P] for u in range(B_UNITS)]
    at += 3 * b_width
    units += [[at + u * P, at + c_width + u * P, at + 2 * c_width + u * P] for u in range(C_UNITS)]
    tiles = []
    for layer in range(DEPTH):
        tiles += [projection(w_in[layer], c) for c in units[0]]
        for u in range(MIX_UNITS):
            if u + 1 < MIX_UNITS:
                tiles += [projection(w_in[layer], c) for c in units[u + 1]]
            tiles.append(w_out[layer, u * P:(u + 1) * P])
        for f in range(F_TILES):
            tiles += [projection(w_up[layer], f * P), projection(w_up[layer], D_FF + f * P)]
            if f:
                tiles.append(w_down[layer, (f - 1) * P:f * P])
        tiles.append(w_down[layer, (F_TILES - 1) * P:])
    return np.stack(tiles)


def dilated_masks():
    d = np.arange(P)[:, None] + SEQ - P - np.arange(SEQ)[None, :]
    held = sum(((d >= 0) & (d % step == 0) & (d <= window)).astype(np.float32) for window, step in DILATED)
    return np.stack([np.where(d >= 0, 0.0, NEG), np.where(held > 0, 0.0, NEG), held], axis=1)


def kernel(x, positions, norm_mix_g, w_in, lambda_q1, lambda_k1, lambda_q2, lambda_k2, subln_g, conv_mix_w,
           w_out, norm_ffn_g, w_up, conv_ffn_w, w_down, final_g):
    import concourse.bacc as bacc
    from concourse.bass_utils import run_bass_kernel_spmd
    import ml_dtypes

    (x, positions, norm_mix_g, w_in, lambda_q1, lambda_k1, lambda_q2, lambda_k2, subln_g, conv_mix_w, w_out,
     norm_ffn_g, w_up, conv_ffn_w, w_down, final_g) = (
        np.asarray(a) for a in (x, positions, norm_mix_g, w_in, lambda_q1, lambda_k1, lambda_q2, lambda_k2,
                                subln_g, conv_mix_w, w_out, norm_ffn_g, w_up, conv_ffn_w, w_down, final_g))

    vectors = np.zeros((P, DEPTH, NV), np.float32)
    for layer in range(DEPTH):
        v = vectors[:, layer]
        v[:, V_FFN_G:V_FFN_G + KT] = by_feature(norm_ffn_g[layer])
        v[:, V_NEXT_G:V_NEXT_G + KT] = by_feature(norm_mix_g[layer + 1] if layer + 1 < DEPTH else final_g)
        for j in range(TAPS):
            v[:, V_CONV_MIX + j:V_CONV_FFN:TAPS] = by_feature(conv_mix_w[layer, j])
            v[:, V_CONV_FFN + j:V_SUBLN:TAPS] = by_feature(conv_ffn_w[layer, j])
        v[:, V_SUBLN] = subln_g[layer]
        for n, a in enumerate((lambda_q1, lambda_k1, lambda_q2, lambda_k2)):
            v[:HEAD_DIM, V_LAMBDA + n] = a[layer]
        lam_init = 0.8 - 0.6 * math.exp(-0.3 * layer)
        v[:, V_LAM_INIT], v[:, V_ONE_LESS] = lam_init, 1.0 - lam_init

    columns = np.zeros((P, 2), np.float32)
    half = ROPE_DIMS // 2
    freq = (np.float32(ROPE_THETA) ** (-(np.arange(half, dtype=np.float32) * np.float32(2.0) / ROPE_DIMS)))
    for start in (0, HEAD_DIM):
        columns[start:start + half] = np.stack([freq, -np.ones(half)], axis=1)
        columns[start + half:start + ROPE_DIMS] = np.stack([freq, np.ones(half)], axis=1)

    arrays = {
        "x_t": np.ascontiguousarray(x[0].T),
        "positions": np.ascontiguousarray(np.broadcast_to(positions, (P, SEQ))),
        "stream": weight_stream(w_in, w_out, w_up, w_down),
        "vectors": vectors.reshape(P, DEPTH * NV),
        "first_g": np.ascontiguousarray(by_feature(norm_mix_g[0])),
        "columns": columns,
        "identity": np.eye(P, dtype=np.float32),
        "masks": dilated_masks().reshape(P, 3 * SEQ).astype(ml_dtypes.bfloat16),
    }
    nc = bacc.Bacc("TRN2", target_bir_lowering=False, num_devices=1)
    ins = [nc.dram_tensor(n, a.shape, mybir.dt.from_np(a.dtype), kind="ExternalInput").ap() for n, a in arrays.items()]
    out = nc.dram_tensor("out_t", (D_MODEL, SEQ), mybir.dt.float32, kind="ExternalOutput").ap()
    build(nc, *ins, out)
    result = run_bass_kernel_spmd(nc, [arrays], core_ids=[0])
    return np.ascontiguousarray(result.results[0]["out_t"].T)[None]
```

```python
import math
from contextlib import ExitStack

import numpy as np

import concourse.bass as bass
import concourse.mybir as mybir

P = 128
D_MODEL = 1024
SEQ = 1024
DEPTH = 2
HEAD_DIM = 64
A_UNITS = D_MODEL // 4 // P
B_UNITS = D_MODEL // 2 // P
C_UNITS = D_MODEL // 4 // P
D_FF = ((8 * D_MODEL // 3 + 127) // 128) * 128
F_TILES = D_FF // P
KT = D_MODEL // P
QB = SEQ // P
HALF = 512
TAPS = 3
DILATED = ((128, 1), (512, 4), (2048, 16))
ROPE_DIMS = HEAD_DIM // 4
ROPE_THETA = 500000.0
CHUNKS = P // ROPE_DIMS
CHUNK = SEQ // CHUNKS
NORM_EPS, SUBLN_EPS = 1e-6, 1e-5
SCALE = HEAD_DIM ** -0.5
NEG = -1e30

MIX_UNITS = A_UNITS + B_UNITS + C_UNITS
LAYER_TILES = 4 * MIX_UNITS + 3 * F_TILES
TILES = DEPTH * LAYER_TILES
W_SLOTS = 2
DOWN_PAIRS = 3

FILLED_AT = (0, 1, 3, 5)
FILLING = ((0, 0), (0, 1), (1, 1), (1, 0))
ROTATE_Q_AT = ((), (), (0, 1), (2,), (3,), (), (), (), ())
ROTATE_K_AT = ((), (), (), (), (), (), (0,), (1,), (2, 3))
ACT_FILLED = (("exps", 1), ("exps", 0), ("keep", 0), ("keep", 1), ("keep", 2), ("keep", 3))
ACT_DILATED = (("keep", 0), ("exps", 1), ("keep", 1), ("keep", 2), ("exps", 0), ("keep", 3))
ACT_DIFFERENTIAL = (("keep", 0), ("exps", 1), ("exps", 0), ("keep", 1))

V_CONV_MIX = 0
V_CONV_FFN = V_CONV_MIX + TAPS * C_UNITS
V_NEG_LAM = V_CONV_FFN + TAPS * F_TILES
V_SUBLN_SCALED = V_NEG_LAM + 1
LAY = V_SUBLN_SCALED + 1
V_FFN_G, V_NEXT_G = LAY, LAY + KT
V_SUBLN = V_NEXT_G + KT
V_LAMBDA = V_SUBLN + 1
V_LAM_INIT = V_LAMBDA + 4
V_ONE_LESS = V_LAM_INIT + 1
NV = V_ONE_LESS + 1

TWO_PI = 2 * math.pi
TURN_A = 6.28125
TURN_B = float(np.float32(int((TWO_PI - TURN_A) * 2 ** 20) / 2 ** 20))
TURN_C = TWO_PI - TURN_A - TURN_B
ROUNDER = 1.5 * 2 ** 23
SIN_END = 3.1415925


class Seen:

    def __init__(self):
        self.count = {}

    def __call__(self, semaphore, n=1):
        self.count[semaphore] = self.count.get(semaphore, 0) + n
        return self.count[semaphore]

    def settle(self, engine):
        for semaphore, n in self.count.items():
            if n:
                engine.wait_ge(semaphore, n).then_inc(semaphore, -n)
                self.count[semaphore] = 0


def build(nc, x_t, positions, stream, vectors, first_g, rope, identity, causal, dilation, out_t):
    f32, f32r, bf16, i32 = (mybir.dt.float32, mybir.dt.float32r, mybir.dt.bfloat16, mybir.dt.int32)
    ALU, ACT = mybir.AluOpType, mybir.ActivationFunctionType
    ctx = ExitStack()
    with ctx:
        def sbuf(name, shape, dtype=f32):
            return ctx.enter_context(nc.sbuf_tensor(name, shape, dtype))

        def sem(name):
            return ctx.enter_context(nc.semaphore(name))

        h = sbuf("h", [P, KT, SEQ])
        x_hi = sbuf("x_hi", [P, KT, SEQ], f32r)
        x_lo = sbuf("x_lo", [P, KT, SEQ], f32r)
        stage = sbuf("stage", [P, W_SLOTS, D_MODEL])
        w_hi = sbuf("w_hi", [P, W_SLOTS, D_MODEL], f32r)
        w_lo = sbuf("w_lo", [P, W_SLOTS, D_MODEL], f32r)
        mix_hi = sbuf("mix_hi", [P, SEQ], f32r)
        mix_lo = sbuf("mix_lo", [P, SEQ], f32r)
        q_split = sbuf("q_split", [P, 2, SEQ], f32r)
        k_twice = sbuf("k_twice", [P, 2, SEQ], f32r)
        k_lo = sbuf("k_lo", [P, SEQ], f32r)
        v_cur = sbuf("v_cur", [P, QB, P])
        q_next, k_next = sbuf("q_next", [P, SEQ]), sbuf("k_next", [P, SEQ])
        v_next = sbuf("v_next", [P, SEQ])
        shuffled = v_next
        prob = sbuf("prob", [P, 2, 2, SEQ])
        heads = sbuf("heads", [P, QB, P])
        rstd_all = sbuf("rstd_all", [P, SEQ])
        padded = sbuf("padded", [P, TAPS - 1 + SEQ])
        cos_t, sin_t = sbuf("cos_t", [P, SEQ]), sbuf("sin_t", [P, SEQ])
        eye = sbuf("eye", [P, P])
        causal_mask = sbuf("causal_mask", [P, SEQ], bf16)
        dilated_mask = sbuf("dilated_mask", [P, SEQ])
        vec = sbuf("vec", [P, DEPTH, NV])
        lay = sbuf("lay", [P, LAY])
        neg_top = sbuf("neg_top", [P, 2, 2])
        total_share = sbuf("total_share", [P, 2, 2, 2])
        total, share = total_share[:, 0, :, :], total_share[:, 1, :, :]
        head_sums = sbuf("head_sums", [P, QB])
        factor = sbuf("factor", [P, 2])
        rs = sbuf("rs", [P, 3, QB])
        ps = ctx.enter_context(nc.psum_tensor("ps", [P, 8, HALF], f32))

        ones = heads[:, 2, :]
        gain = heads[:, 3, 0:KT]
        taps = heads[:, 4, 0:2 * TAPS]
        turn_by = heads[:, 5, 0:2]
        lam, lam_exp = heads[:, 6, 0:2 * DEPTH], heads[:, 7, 0:2 * DEPTH]
        squares = (q_next[:, :], k_next[:, :], v_next[:, :], v_cur[:, :, :].rearrange("p b d -> p (b d)"),
                   padded[:, TAPS - 1:], prob[:, 0, 1, :], prob[:, 1, 0, :], prob[:, 1, 1, :])
        diagonal = prob[:, 0, 0, :]
        second = (prob[:, 0, 0, :], prob[:, 0, 1, :], prob[:, 1, 0, :])
        gated = prob[:, 1, 1, :]
        place, angle, turns = (v_cur[:, n, :] for n in range(3))
        sine, cosine = heads[:, 0, :], heads[:, 1, :]

        def bank(b, n=1):
            return ps[:, b:b + n, :].rearrange("p b t -> p (b t)")

        PROJ, SCORE, TURNED, HEAD = 0, 2, 6, 7
        DOWN = SCORE
        turned_groups = (padded[:, TAPS - 1:TAPS - 1 + HALF], padded[:, TAPS - 1 + HALF:])

        def turned_bank(i, n):
            return PROJ + 1 if i >= QB // 2 and n % 2 else TURNED

        SPARE = SCORE + 2

        stage_full = [sem(f"stage_full{s}") for s in range(W_SLOTS)]
        stage_free = sem("stage_free")
        w_ready, w_free = sem("w_ready"), sem("w_free")
        pool_seq = sem("pool_seq")
        vectors_in, gain_in = sem("vectors_in"), sem("gain_in")
        eye_in, masks_in = sem("eye_in"), sem("masks_in")
        pos_in, tables_in = sem("pos_in"), sem("tables_in")
        x_in = [sem(f"x_in{m}") for m in range(KT)]
        lam_ready = sem("lam_ready")
        dve_seq, act_seq = sem("dve_seq"), sem("act_seq")
        x_lo_ready = sem("x_lo_ready")
        half_done, half_free = sem("half_done"), sem("half_free")
        down_done, down_free = sem("down_done"), sem("down_free")
        mix_ready = sem("mix_ready")
        h_new = sem("h_new")
        x_hi_ready, x_hi_kept = sem("x_hi_ready"), sem("x_hi_kept")
        squares_ready, pairs_ready = sem("squares_ready"), sem("pairs_ready")
        partial_ready = sem("partial_ready")
        sum_done = sem("sum_done")
        diag_ready = sem("diag_ready")
        spread_done = sem("spread_done")
        rstd_ready = sem("rstd_ready")
        cur_ready = sem("cur_ready")
        next_ready, next_kept = sem("next_ready"), sem("next_kept")
        v_ready, v_turned = sem("v_ready"), sem("v_turned")
        v_kept = sem("v_kept")
        score_done, score_free = sem("score_done"), sem("score_free")
        top_ready, exp_done = sem("top_ready"), sem("exp_done")
        share_ready = sem("share_ready")
        prob_ready, prob_free = sem("prob_ready"), sem("prob_free")
        turned_done, turned_out = sem("turned_done"), sem("turned_out")
        head_done, head_free = sem("head_done"), sem("head_free")
        head_sums_ready = sem("head_sums_ready")
        heads_ready = sem("heads_ready")
        heads_turned = sem("heads_turned")
        value_ready, hi_ready = sem("value_ready"), sem("hi_ready")
        gate_ready, gate_used = sem("gate_ready"), sem("gate_used")
        conv_ready, silu_done = sem("conv_ready"), sem("silu_done")
        angle_ready, tables_free = sem("angle_ready"), sem("tables_free")
        lam_summed = sem("lam_summed")
        lam_exped = sem("lam_exped")
        out_ready, out_done = sem("out_ready"), sem("out_done")

        block = ctx.enter_context(nc.Block())

        @block.sync
        def _(sp):
            seen = Seen()
            sp.dma_start(vec[:, :, :].rearrange("p l v -> p (l v)"), vectors).then_inc(vectors_in, 16)
            rounds = stream.rearrange("(r s) p n -> r s p n", s=W_SLOTS)
            with sp.Fori(0, TILES // W_SLOTS) as r:
                for s in range(W_SLOTS):
                    sp.wait_ge(stage_free, seen(stage_free))
                    sp.dma_start(stage[:, s, :], rounds[bass.ds(r, 1), s, :, :].rearrange("o p n -> (o p) n"))\
                      .then_inc(stage_full[s], 16)
                seen.settle(sp)
            for m in range(KT):
                sp.wait_ge(out_ready, m + 1)
                sp.dma_start(out_t[m * P:(m + 1) * P, :], h[:, m, :]).then_inc(out_done, 16)
            sp.wait_ge(out_done, 16 * KT)

        @block.gpsimd
        def _(pool):
            seen = Seen()

            def split(s):
                pool.wait_ge(stage_full[s], seen(stage_full[s], 16))
                pool.wait_ge(w_free, seen(w_free))
                pool.tensor_copy(w_hi[:, s, :], stage[:, s, :]).then_inc(pool_seq, 1)
                pool.wait_ge(pool_seq, seen(pool_seq))
                pool.tensor_tensor(w_lo[:, s, :], stage[:, s, :], w_hi[:, s, :].bitcast(f32), ALU.subtract)\
                    .then_inc(pool_seq, 1)
                pool.wait_ge(pool_seq, seen(pool_seq))
                pool.sem_inc(w_ready, 1)
                pool.sem_inc(stage_free, 1)

            def add_squares(m, other):
                pool.tensor_tensor(squares[m], squares[m], squares[other], ALU.add).then_inc(pool_seq, 1)
                pool.wait_ge(pool_seq, seen(pool_seq))

            def start_sums():
                for m in (0, 2, 4):
                    pool.wait_ge(squares_ready, seen(squares_ready, 2))
                    add_squares(m, m + 1)

            def end_sums():
                pool.wait_ge(squares_ready, seen(squares_ready, 2))
                add_squares(6, 7)
                add_squares(0, 2)
                pool.sem_inc(pairs_ready, 1)

            def sublayer(tiles, last=False):
                start_sums()
                split(1)
                end_sums()
                seen.settle(pool)
                with pool.Fori(0, (tiles - 2) // W_SLOTS):
                    for s in range(W_SLOTS):
                        split(s)
                    seen.settle(pool)
                if not last:
                    split(0)

            pool.sem_inc(stage_free, W_SLOTS)
            split(0)
            seen.settle(pool)
            with pool.Fori(0, DEPTH - 1):
                sublayer(4 * MIX_UNITS)
                sublayer(3 * F_TILES)
                seen.settle(pool)
            sublayer(4 * MIX_UNITS)
            sublayer(3 * F_TILES, last=True)
            start_sums()
            end_sums()

        @block.tensor
        def _(pe):
            seen = Seen()
            slot = [0]

            def next_slot():
                s = slot[0]
                slot[0] = (s + 1) % W_SLOTS
                return s

            def three_pass(out, slices, moving, start, stop):
                (s, w), (hi, lo) = slices, moving
                first = pe.matmul(out, w_hi[:, s, w], hi, start=start, stop=False)
                pe.matmul(out, w_hi[:, s, w], lo, start=False, stop=False)
                return first, pe.matmul(out, w_lo[:, s, w], hi, start=False, stop=stop)

            def project_half(s, n, opens):
                t = slice(n * HALF, (n + 1) * HALF)
                if opens:
                    pe.wait_ge(w_ready, seen(w_ready))
                pe.wait_ge(half_free, seen(half_free))
                for k in range(KT):
                    begun, last = three_pass(bank(PROJ + n), (s, slice(k * P, (k + 1) * P)),
                                             (x_hi[:, k, t], x_lo[:, k, t]), k == 0, k == KT - 1)
                    if opens and k == 0:
                        begun.then_inc(w_free, 1)
                last.then_inc(half_done, 1)

            def project():
                s = next_slot()
                for n in range(2):
                    project_half(s, n, n == 0)

            def down(last=False):
                pairs = 2 if last else DOWN_PAIRS
                s = next_slot()
                pe.wait_ge(w_ready, seen(w_ready))
                pe.wait_ge(mix_ready, seen(mix_ready))
                if last:
                    pe.wait_ge(down_free, seen(down_free))
                for m in range(KT):
                    pe.wait_ge(down_free, seen(down_free))
                    for n in range(2):
                        t = slice(n * HALF, (n + 1) * HALF)
                        begun, ended = three_pass(bank(DOWN + 2 * (m % pairs) + n), (s, slice(m * P, (m + 1) * P)),
                                                  (mix_hi[:, t], mix_lo[:, t]), True, True)
                        if m == 0 and n == 0:
                            begun.then_inc(w_free, 1)
                    ended.then_inc(down_done, 1)
                if last:
                    pe.sem_inc(down_free, 1)

            def sum_squares():
                pe.wait_ge(partial_ready, seen(partial_ready))
                for b in range(QB):
                    last = pe.matmul(ps[:, HEAD, b:b + 1], squares[0][:, b * P:(b + 1) * P], ones[:, 0:1],
                                     start=True, stop=True)
                last.then_inc(sum_done, 1)

            def spread():
                pe.wait_ge(diag_ready, seen(diag_ready))
                for n in range(2):
                    last = pe.matmul(bank(SCORE + n), ones[:, :], diagonal[:, n * HALF:(n + 1) * HALF],
                                     start=True, stop=True)
                last.then_inc(spread_done, 1)

            def start_normed():
                slots = (next_slot(), next_slot())
                banks = (PROJ, SPARE)
                pe.wait_ge(half_free, seen(half_free, 2))
                for s, first_bank in zip(slots, banks):
                    pe.wait_ge(w_ready, seen(w_ready))
                    for k in range(KT):
                        w = slice(k * P, (k + 1) * P)
                        if s == slots[0]:
                            pe.wait_ge(x_hi_ready, seen(x_hi_ready))
                        for n in range(2):
                            t = slice(n * HALF, (n + 1) * HALF)
                            begun = pe.matmul(bank(first_bank + n), w_hi[:, s, w], x_hi[:, k, t],
                                              start=k == 0, stop=False)
                            if s == slots[0] and k == 0 and n == 0:
                                begun.then_inc(w_free, 1)
                            pe.matmul(bank(first_bank + n), w_lo[:, s, w], x_hi[:, k, t], start=False, stop=False)
                sum_squares()
                for s, first_bank in zip(slots, banks):
                    for k in range(KT):
                        w = slice(k * P, (k + 1) * P)
                        if s == slots[0]:
                            pe.wait_ge(x_lo_ready, seen(x_lo_ready))
                        for n in range(2):
                            last = pe.matmul(bank(first_bank + n), w_hi[:, s, w], x_lo[:, k, n * HALF:(n + 1) * HALF],
                                             start=False, stop=k == KT - 1)
                            if k == KT - 1:
                                last.then_inc(half_done, 1)
                            elif s == slots[1] and k == 0 and n == 0:
                                last.then_inc(w_free, 1)
                spread()

            def scores(i, j):
                if i == 0 and j == 1:
                    pe.wait_ge(cur_ready, seen(cur_ready))
                pe.wait_ge(score_free, seen(score_free))
                keys = (i + 1) * P
                rows, queries = slice(HEAD_DIM * j, HEAD_DIM * (j + 1)), slice(i * P, (i + 1) * P)
                for n in range(0, keys, HALF):
                    wide = min(HALF, keys - n)
                    out = ps[:, SCORE + 2 * j + n // HALF, 0:wide]
                    pe.matmul(out, q_split[:, j, queries], k_twice[:, j, n:n + wide], start=True, stop=False)
                    last = pe.matmul(out, q_split[rows, j, queries], k_lo[rows, n:n + wide], start=False, stop=True)
                last.then_inc(score_done, 1)

            def turn(source, blocks, to):
                for b in range(blocks):
                    last = pe.transpose(ps[:, to, b * P:(b + 1) * P], source[:, b * P:(b + 1) * P], eye[:, :])
                last.then_inc(turned_done, 1)

            def groups(i, dilated):
                return [(j, b, min(4, i + 1 - b)) for j in ((1, 0) if dilated else (0,)) for b in range(0, i + 1, 4)]

            def turn_group(i, dilated, n):
                j, b, blocks = groups(i, dilated)[n]
                if n == 0 or j != groups(i, dilated)[n - 1][0]:
                    pe.wait_ge(prob_ready, seen(prob_ready))
                turn(prob[:, i % 2, j, b * P:], blocks, turned_bank(i, n))

            def ahead(i):
                return 2 if i >= QB // 2 else 1

            def start_attend(i, dilated):
                if i == QB // 2:
                    read = 1 if i + 1 in FILLED_AT else 2
                    pe.wait_ge(half_free, seen(half_free, read))
                    pe.sem_inc(half_free, read)
                for n in range(ahead(i)):
                    turn_group(i, dilated, n)

            def end_attend(i, dilated):
                todo = groups(i, dilated)
                pe.wait_ge(head_free, seen(head_free))
                for n, (j, b0, blocks) in enumerate(todo):
                    pe.wait_ge(turned_out, seen(turned_out))
                    if n + ahead(i) < len(todo) and ahead(i) == 1:
                        turn_group(i, dilated, n + 1)
                    for b in range(b0, b0 + blocks):
                        keys = slice((b - b0) * P, (b - b0 + 1) * P)
                        last = pe.matmul(ps[:, HEAD, j * P:(j + 1) * P], turned_groups[n % 2][:, keys],
                                         v_cur[:, b, :], start=b == 0, stop=b == i)
                    if n + ahead(i) < len(todo) and ahead(i) == 2:
                        turn_group(i, dilated, n + 2)
                last.then_inc(head_done, 1)

            def turn_v():
                pe.wait_ge(v_ready, seen(v_ready))
                for b in range(QB):
                    last = pe.transpose(ps[:, TURNED + b // 4, (b % 4) * P:(b % 4 + 1) * P],
                                        v_next[:, b * P:(b + 1) * P], eye[:, :])
                last.then_inc(v_turned, 1)

            def turn_heads():
                pe.wait_ge(heads_ready, seen(heads_ready))
                for b in range(QB):
                    last = pe.transpose(ps[:, SCORE + b // 4, (b % 4) * P:(b % 4 + 1) * P], heads[:, b, :], eye[:, :])
                last.then_inc(heads_turned, 1)

            def unit(dilated):
                for i in range(QB):
                    if i == 0:
                        s = next_slot()
                        project_half(s, 0, True)
                        turn_v()
                    scores(i, 1)
                    scores(i, 0)
                    if i and i in FILLED_AT:
                        half = FILLED_AT.index(i)
                        s = s if half % 2 else next_slot()
                        project_half(s, FILLING[half][1], half % 2 == 0)
                    if i == 1:
                        pe.wait_ge(v_kept, seen(v_kept))
                    if i:
                        start_attend(i - 1, dilated)
                        end_attend(i - 1, dilated)
                start_attend(QB - 1, dilated)
                end_attend(QB - 1, dilated)
                s = next_slot()
                project_half(s, 0, True)
                turn_heads()
                project_half(s, 1, False)
                down()

            pe.wait_ge(lam_ready, seen(lam_ready))
            pe.matmul(ps[:, TURNED, 0:2 * DEPTH], ones[:, :], lam[:, :], start=True, stop=True).then_inc(lam_summed, 1)
            pe.wait_ge(eye_in, 16)
            seen.settle(pe)
            with pe.Fori(0, DEPTH):
                start_normed()
                project()
                seen.settle(pe)
                with pe.Fori(0, A_UNITS):
                    unit(True)
                    seen.settle(pe)
                with pe.Fori(0, B_UNITS - 1):
                    unit(False)
                    seen.settle(pe)
                unit(False)
                for _ in range(3):
                    project()
                down()
                down(last=True)
                start_normed()
                project()
                project()
                down()
                seen.settle(pe)
                with pe.Fori(0, (F_TILES - 2) // 2):
                    for _ in range(2):
                        project()
                        project()
                        down()
                    seen.settle(pe)
                down(last=True)
                seen.settle(pe)
            sum_squares()
            spread()

        @block.scalar
        def _(act):
            seen = Seen()

            def square_tile(m, loaded):
                if loaded:
                    act.wait_ge(x_in[m], 16)
                else:
                    act.wait_ge(h_new, seen(h_new))
                act.activation(squares[m], h[:, m, :], ACT.Square).then_inc(squares_ready, 1)

            def head_tile(m):
                act.activation(x_hi[:, m, :], h[:, m, :], ACT.Copy, scale=gain[:, m:m + 1]).then_inc(act_seq, 1)
                act.wait_ge(act_seq, seen(act_seq))
                act.sem_inc(x_hi_ready, 1)
                act.sem_inc(x_hi_kept, 1)

            def prepare(loaded=False):
                for m in range(KT):
                    square_tile(m, loaded)
                    if KT // 2 <= m < KT - 1:
                        head_tile(m - KT // 2)
                for m in range(KT // 2 - 1, KT):
                    head_tile(m)

            def keep_rstd():
                act.wait_ge(spread_done, seen(spread_done))
                act.activation(rstd_all[:, :], bank(SCORE, 2), ACT.Copy).then_inc(rstd_ready, 1)

            def keep_turned(i, n, size):
                act.wait_ge(turned_done, seen(turned_done))
                act.activation(turned_groups[n % 2][:, 0:size], ps[:, turned_bank(i, n), 0:size], ACT.Copy)\
                   .then_inc(turned_out, 1)

            def keep_v():
                act.wait_ge(v_turned, seen(v_turned))
                act.activation(v_cur[:, :, :].rearrange("p b d -> p (b d)"), bank(TURNED, 2), ACT.Copy)\
                   .then_inc(v_kept, 1)

            def keep_next():
                low, high = slice(0, HEAD_DIM), slice(HEAD_DIM, P)
                for new, copies in ((q_next, ((low, q_split[low, 0, :]), (high, q_split[high, 1, :]))),
                                    (k_next, ((low, k_twice[low, 0, :]), (low, k_twice[high, 0, :]),
                                              (high, k_twice[low, 1, :]), (high, k_twice[high, 1, :])))):
                    act.wait_ge(next_ready, seen(next_ready))
                    for rows, out in copies:
                        act.activation(out, new[rows, :], ACT.Copy).then_inc(act_seq, 1)
                    act.wait_ge(act_seq, seen(act_seq, len(copies)))
                    act.sem_inc(next_kept, 1)

            def keep_head(i, dilated):
                act.wait_ge(head_done, seen(head_done))
                act.wait_ge(share_ready, seen(share_ready))
                if dilated:
                    for j in range(2):
                        dims = slice(HEAD_DIM * j, HEAD_DIM * (j + 1))
                        own = slice(j * P + dims.start, j * P + dims.stop)
                        act.activation(heads[:, i, dims], ps[:, HEAD, own], ACT.Copy, scale=share[:, i % 2, j:j + 1])\
                           .then_inc(act_seq, 1)
                else:
                    act.activation(heads[:, i, :], ps[:, HEAD, 0:P], ACT.Copy, scale=share[:, i % 2, 0:1])\
                       .then_inc(act_seq, 1)
                    act.activation(ps[:, HEAD, P:2 * P], ps[:, HEAD, 0:P], ACT.Square, scale=share[:, i % 2, 0:1],
                                   accum_out=head_sums[:, i:i + 1]).then_inc(act_seq, 1)
                act.wait_ge(act_seq, seen(act_seq, 2))
                act.sem_inc(head_free, 1)

            def exps(i, j, dilated):
                scores = prob[:, i % 2, j, 0:(i + 1) * P]
                act.wait_ge(top_ready, seen(top_ready))
                bias, sums = neg_top[:, i % 2, j:j + 1], total[:, i % 2, j:j + 1]
                if dilated:
                    act.activation(scores, scores, ACT.Exp, bias=bias, scale=-1.0, accum_out=sums).then_inc(act_seq, 1)
                    act.wait_ge(act_seq, seen(act_seq))
                    act.sem_inc(prob_ready, 1)
                    act.sem_inc(exp_done, 1)
                else:
                    act.activation(scores, scores, ACT.Exp, bias=bias, scale=-1.0, accum_out=sums).then_inc(exp_done, 1)

            def keep_hi(source):
                act.wait_ge(value_ready, seen(value_ready))
                act.activation(mix_hi[:, :], source, ACT.Copy).then_inc(hi_ready, 1)

            def unit(dilated, next_attends=True):
                keep_v()
                exps(0, 1, dilated)
                exps(0, 0, dilated)
                for i in range(QB):
                    sizes = [min(4, i + 1 - b) for _ in range(2 if dilated else 1) for b in range(0, i + 1, 4)]
                    bare = ACT_DILATED if dilated else ACT_DIFFERENTIAL
                    for kind, n in (ACT_FILLED if i + 1 in FILLED_AT else bare):
                        if kind == "keep" and n < len(sizes):
                            keep_turned(i, n, sizes[n] * P)
                        if kind == "exps" and i + 1 < QB:
                            exps(i + 1, n, dilated)
                    act.wait_ge(turned_done, seen.count[turned_done]).then_inc(prob_free, 1)
                    keep_head(i, dilated)
                act.sem_inc(heads_ready if dilated else head_sums_ready, 1)
                if next_attends:
                    keep_next()
                act.wait_ge(heads_turned, seen(heads_turned))
                head_gain = 1.0 if dilated else lay[:, V_SUBLN_SCALED:V_SUBLN_SCALED + 1]
                act.activation(mix_hi[:, :], bank(SCORE, 2), ACT.Copy, scale=head_gain).then_inc(hi_ready, 1)

            def conv_center(out, tap):
                act.wait_ge(gate_ready, seen(gate_ready))
                act.activation(out, padded[:, TAPS - 1:], ACT.Copy, scale=tap).then_inc(gate_used, 1)

            def hidden(f):
                conv_center(k_next[:, :], taps[:, TAPS * (f % 2) + 2:TAPS * (f % 2) + 3])
                act.wait_ge(conv_ready, seen(conv_ready))
                act.activation(k_next[:, :], k_next[:, :], ACT.Silu).then_inc(silu_done, 1)
                keep_hi(k_next[:, :])

            act.sem_inc(head_free, 1)
            act.dma_start(place.bitcast(i32), positions).then_inc(pos_in, 16)
            act.dma_start(turn_by[:, :], rope).then_inc(pos_in, 16)
            act.dma_start(gain[:, :], first_g).then_inc(gain_in, 16)
            for m in range(KT):
                act.dma_start(h[:, m, :], x_t[m * P:(m + 1) * P, :]).then_inc(x_in[m], 16)
            act.dma_start(eye[:, :], identity).then_inc(eye_in, 16)
            act.dma_start(causal_mask[:, :], causal).then_inc(masks_in, 16)
            act.dma_start(dilated_mask[:, :], dilation).then_inc(masks_in, 16)
            act.wait_ge(angle_ready, seen(angle_ready))
            for wave, out in ((turns, sine), (place, cosine)):
                act.activation(out, wave, ACT.Sin).then_inc(act_seq, 1)
                act.wait_ge(act_seq, seen(act_seq))
            act.wait_ge(lam_summed, seen(lam_summed))
            act.activation(lam_exp[:, :], ps[:, TURNED, 0:2 * DEPTH], ACT.Exp).then_inc(lam_exped, 1)
            act.wait_ge(gain_in, 16)
            prepare(loaded=True)
            act.wait_ge(tables_free, 1)
            for head in (0, HEAD_DIM):
                for table, source in ((sin_t, sine), (cos_t, cosine)):
                    act.dma_start(table[head:head + ROPE_DIMS, :], source).then_inc(tables_in, 16)
            seen.settle(act)
            with act.Fori(0, DEPTH):
                keep_rstd()
                keep_next()
                seen.settle(act)
                with act.Fori(0, A_UNITS):
                    unit(True)
                    seen.settle(act)
                with act.Fori(0, B_UNITS - 1):
                    unit(False)
                    seen.settle(act)
                unit(False, next_attends=False)
                for u, out in enumerate((k_next[:, :], second[1])):
                    conv_center(out, lay[:, V_CONV_MIX + TAPS * u + 2:V_CONV_MIX + TAPS * u + 3])
                    keep_hi(gated)
                prepare()
                keep_rstd()
                hidden(0)
                hidden(1)
                seen.settle(act)
                with act.Fori(0, (F_TILES - 2) // 2):
                    hidden(0)
                    hidden(1)
                    seen.settle(act)
                prepare()
                seen.settle(act)
            keep_rstd()

        @block.vector
        def _(dve):
            seen = Seen()

            def evacuate(n, out, first_bank=PROJ):
                t = slice(n * HALF, (n + 1) * HALF)
                dve.wait_ge(half_done, seen(half_done))
                dve.tensor_tensor(out[:, t], bank(first_bank + n), rstd_all[:, t], ALU.mult).then_inc(dve_seq, 1)
                dve.wait_ge(dve_seq, seen(dve_seq))
                if first_bank == PROJ:
                    dve.sem_inc(half_free, 1)

            def absorb():
                for m in range(KT):
                    dve.wait_ge(x_hi_kept, seen(x_hi_kept))
                    dve.scalar_tensor_tensor(x_lo[:, m, :], h[:, m, :], gain[:, m:m + 1], x_hi[:, m, :].bitcast(f32),
                                             ALU.mult, ALU.subtract).then_inc(dve_seq, 1)
                    dve.wait_ge(dve_seq, seen(dve_seq))
                    dve.sem_inc(x_lo_ready, 1)

            def add_down(m, pairs=DOWN_PAIRS):
                dve.wait_ge(down_done, seen(down_done))
                dve.tensor_tensor(h[:, m, :], bank(DOWN + 2 * (m % pairs), 2), h[:, m, :], ALU.add)\
                   .then_inc(dve_seq, 1)
                dve.wait_ge(dve_seq, seen(dve_seq))
                dve.sem_inc(down_free, 1)

            def add_last_down(layer, g):
                dve.tensor_copy(gain[:, :], vec[:, bass.ds(layer, 1), g:g + KT].rearrange("p o v -> p (o v)"))\
                   .then_inc(dve_seq, 1)
                dve.wait_ge(dve_seq, seen(dve_seq))
                for m in range(KT):
                    add_down(m, 2)
                    dve.sem_inc(h_new, 1)

            def rsqrt(sums, width, eps):
                mean, y, t = rs[:, 0, :], rs[:, 1, :], rs[:, 2, :]
                dve.tensor_scalar(mean, sums, 1.0 / width, eps, ALU.mult, ALU.add).then_inc(dve_seq, 1)
                dve.wait_ge(dve_seq, seen(dve_seq))
                dve.tensor_scalar(y.bitcast(i32), mean.bitcast(i32), 1, None, ALU.arith_shift_right)\
                   .then_inc(dve_seq, 1)
                dve.wait_ge(dve_seq, seen(dve_seq))
                dve.tensor_scalar(y.bitcast(i32), y.bitcast(i32), -1.0, float(0x5F3759DF), ALU.mult, ALU.add)\
                   .then_inc(dve_seq, 1)
                dve.wait_ge(dve_seq, seen(dve_seq))
                for _ in range(3):
                    dve.scalar_tensor_tensor(t, y, -0.5, y, ALU.mult, ALU.mult).then_inc(dve_seq, 1)
                    dve.wait_ge(dve_seq, seen(dve_seq))
                    dve.tensor_tensor(t, t, mean, ALU.mult).then_inc(dve_seq, 1)
                    dve.wait_ge(dve_seq, seen(dve_seq))
                    dve.scalar_tensor_tensor(y, t, 1.5, y, ALU.add, ALU.mult).then_inc(dve_seq, 1)
                    dve.wait_ge(dve_seq, seen(dve_seq))
                return y

            def start_norm():
                dve.memset(ones[:, :], 1.0).then_inc(dve_seq, 1)
                dve.wait_ge(dve_seq, seen(dve_seq))
                dve.wait_ge(pairs_ready, seen(pairs_ready))
                for m, other in ((4, 6), (0, 4)):
                    dve.tensor_tensor(squares[m], squares[m], squares[other], ALU.add).then_inc(dve_seq, 1)
                    dve.wait_ge(dve_seq, seen(dve_seq))
                dve.sem_inc(partial_ready, 1)
                dve.wait_ge(sum_done, seen(sum_done))
                y = rsqrt(ps[:, HEAD, 0:QB], D_MODEL, NORM_EPS)
                blocks = [P, QB, P]
                dve.tensor_tensor(diagonal.rearrange("p (b q) -> p b q", q=P),
                                  eye[:, :].unsqueeze(1).broadcast_to(blocks), y.unsqueeze(2).broadcast_to(blocks),
                                  ALU.mult).then_inc(dve_seq, 1)
                dve.wait_ge(dve_seq, seen(dve_seq))
                dve.sem_inc(diag_ready, 1)
                dve.wait_ge(rstd_ready, seen(rstd_ready))

            def rotate(x, steps=range(4)):
                swap = [p ^ (ROPE_DIMS // 2) for p in range(32)]
                for step in steps:
                    if step == 0:
                        dve.stream_shuffle(shuffled[:, :], x[:, :], swap).then_inc(dve_seq, 1)
                    elif step == 1:
                        dve.tensor_tensor(shuffled[:, :], shuffled[:, :], sin_t[:, :], ALU.mult).then_inc(dve_seq, 1)
                    elif step == 2:
                        dve.tensor_tensor(x[:, :], x[:, :], cos_t[:, :], ALU.mult).then_inc(dve_seq, 1)
                    else:
                        dve.tensor_tensor(x[:, :], x[:, :], shuffled[:, :], ALU.add).then_inc(dve_seq, 1)
                    dve.wait_ge(dve_seq, seen(dve_seq))
                    if step == 3:
                        dve.sem_inc(next_ready, 1)

            def split_next():
                low, high = slice(0, HEAD_DIM), slice(HEAD_DIM, P)
                for new, rests in ((q_next, ((low, q_split[low, 0, :], q_split[high, 0, :]),
                                             (high, q_split[high, 1, :], q_split[low, 1, :]))),
                                   (k_next, ((low, k_twice[low, 0, :], k_lo[low, :]),
                                             (high, k_twice[high, 1, :], k_lo[high, :])))):
                    dve.wait_ge(next_kept, seen(next_kept))
                    for rows, head, rest in rests:
                        dve.tensor_tensor(rest, new[rows, :], head.bitcast(f32), ALU.subtract).then_inc(dve_seq, 1)
                    dve.wait_ge(dve_seq, seen(dve_seq, len(rests)))
                dve.sem_inc(cur_ready, 1)

            def tops(i, dilated):
                keys, at = (i + 1) * P, i % 2
                mask = dilated_mask if dilated else causal_mask
                if i >= 2:
                    dve.wait_ge(prob_free, seen(prob_free))
                for j in (1, 0):
                    dve.wait_ge(score_done, seen(score_done))
                    dve.tensor_tensor_reduce(out=prob[:, at, j, 0:keys], in0=bank(SCORE + 2 * j, 2)[:, 0:keys],
                                             in1=mask[:, SEQ - keys:SEQ], scale=-SCALE,
                                             scalar=3e38, op0=ALU.add, op1=ALU.min,
                                             accum_out=neg_top[:, at, j:j + 1]).then_inc(dve_seq, 1)
                    dve.wait_ge(dve_seq, seen(dve_seq))
                    dve.sem_inc(top_ready, 1)
                    if i < QB - 1:
                        dve.sem_inc(score_free, 1)

            def invert(i):
                dve.wait_ge(exp_done, seen(exp_done, 2))
                dve.reciprocal(share[:, i % 2, :], total[:, i % 2, :]).then_inc(dve_seq, 1)
                dve.wait_ge(dve_seq, seen(dve_seq))
                dve.sem_inc(share_ready, 1)

            def subtract(i):
                keys, at = (i + 1) * P, i % 2
                p0, p1 = prob[:, at, 0, 0:keys], prob[:, at, 1, 0:keys]
                dve.scalar_tensor_tensor(factor[:, at:at + 1], share[:, at, 1:2], lay[:, V_NEG_LAM:V_NEG_LAM + 1],
                                         total[:, at, 0:1], ALU.mult, ALU.mult).then_inc(dve_seq, 1)
                dve.wait_ge(dve_seq, seen(dve_seq))
                dve.scalar_tensor_tensor(p0, p1, factor[:, at:at + 1], p0, ALU.mult, ALU.add).then_inc(prob_ready, 1)

            def keep_lo(source, gain=1.0):
                dve.wait_ge(hi_ready, seen(hi_ready))
                dve.scalar_tensor_tensor(mix_lo[:, :], source, gain, mix_hi[:, :].bitcast(f32),
                                         ALU.mult, ALU.subtract).then_inc(dve_seq, 1)
                dve.wait_ge(dve_seq, seen(dve_seq))
                dve.sem_inc(mix_ready, 1)

            def unit(dilated, next_attends=True):
                for i in range(QB):
                    tops(i, dilated)
                    if next_attends:
                        rotate(q_next, ROTATE_Q_AT[i])
                        rotate(k_next, ROTATE_K_AT[i])
                    invert(i)
                    if not dilated:
                        subtract(i)
                    if i in FILLED_AT:
                        x, n = FILLING[FILLED_AT.index(i)]
                        evacuate(n, (q_next, k_next)[x])
                if next_attends:
                    rotate(k_next, ROTATE_K_AT[QB])
                dve.wait_ge(prob_free, seen(prob_free, 2))
                if not dilated:
                    dve.wait_ge(head_sums_ready, seen(head_sums_ready))
                    y = rsqrt(head_sums[:, :], P, SUBLN_EPS)
                    for b in range(QB):
                        dve.tensor_scalar(heads[:, b, :], heads[:, b, :], y[:, b:b + 1], None, ALU.mult)\
                           .then_inc(dve_seq, 1)
                    dve.wait_ge(dve_seq, seen(dve_seq, QB))
                    dve.sem_inc(heads_ready, 1)
                if next_attends:
                    split_next()
                evacuate(0, v_next)
                if dilated:
                    keep_lo(bank(SCORE, 2))
                else:
                    keep_lo(bank(SCORE, 2), lay[:, V_SUBLN_SCALED:V_SUBLN_SCALED + 1])
                evacuate(1, v_next)
                for m in range(KT):
                    add_down(m)
                if next_attends:
                    dve.sem_inc(v_ready, 1)
                    dve.sem_inc(score_free, 2)

            def conv_taps(out, tap):
                dve.wait_ge(gate_used, seen(gate_used))
                for back in (1, 2):
                    dve.scalar_tensor_tensor(out[:, :], padded[:, TAPS - 1 - back:TAPS - 1 - back + SEQ],
                                             tap(TAPS - 1 - back), out[:, :], ALU.mult, ALU.add).then_inc(dve_seq, 1)
                    dve.wait_ge(dve_seq, seen(dve_seq))

            def hidden(f, down=True, up_bank=PROJ):
                for n in range(2):
                    evacuate(n, padded[:, TAPS - 1:])
                dve.sem_inc(gate_ready, 1)
                conv_taps(k_next, lambda j: taps[:, TAPS * (f % 2) + j:TAPS * (f % 2) + j + 1])
                dve.sem_inc(conv_ready, 1)
                for n in range(2):
                    evacuate(n, q_next, up_bank)
                if down:
                    for m in range(KT):
                        add_down(m)
                dve.wait_ge(silu_done, seen(silu_done))
                dve.tensor_tensor(k_next[:, :], k_next[:, :], q_next[:, :], ALU.mult).then_inc(dve_seq, 1)
                dve.wait_ge(dve_seq, seen(dve_seq))
                dve.sem_inc(value_ready, 1)
                keep_lo(k_next[:, :])

            dve.memset(ones[:, :], 1.0).then_inc(dve_seq, 1)
            dve.wait_ge(dve_seq, seen(dve_seq))
            dve.memset(padded[:, 0:TAPS - 1], 0.0).then_inc(dve_seq, 1)
            dve.wait_ge(dve_seq, seen(dve_seq))
            dve.memset(sin_t[:, :], 0.0).then_inc(dve_seq, 1)
            dve.wait_ge(dve_seq, seen(dve_seq))
            dve.memset(cos_t[:, :], 1.0).then_inc(dve_seq, 1)
            dve.wait_ge(dve_seq, seen(dve_seq))
            dve.sem_inc(tables_free, 1)
            dve.sem_inc(half_free, 2)
            dve.sem_inc(down_free, DOWN_PAIRS)
            dve.sem_inc(w_free, 1)
            dve.wait_ge(vectors_in, 16)
            for layer in range(DEPTH):
                for n in range(2):
                    c = V_LAMBDA + 2 * n
                    dve.tensor_tensor(lam[:, 2 * layer + n:2 * layer + n + 1], vec[:, layer, c:c + 1],
                                      vec[:, layer, c + 1:c + 2], ALU.mult).then_inc(dve_seq, 1)
                    dve.wait_ge(dve_seq, seen(dve_seq))
            dve.sem_inc(lam_ready, 1)
            dve.wait_ge(pos_in, 32)
            dve.tensor_copy(angle, place.bitcast(i32)).then_inc(dve_seq, 1)
            dve.wait_ge(dve_seq, seen(dve_seq))
            dve.tensor_scalar(angle, angle, turn_by[:, 0:1], None, ALU.mult).then_inc(dve_seq, 1)
            dve.wait_ge(dve_seq, seen(dve_seq))
            dve.tensor_scalar(turns, angle, 1 / TWO_PI, None, ALU.mult).then_inc(dve_seq, 1)
            dve.wait_ge(dve_seq, seen(dve_seq))
            dve.tensor_scalar(turns, turns, ROUNDER, None, ALU.add).then_inc(dve_seq, 1)
            dve.wait_ge(dve_seq, seen(dve_seq))
            dve.tensor_scalar(turns, turns, -ROUNDER, None, ALU.add).then_inc(dve_seq, 1)
            dve.wait_ge(dve_seq, seen(dve_seq))
            for part in (TURN_A, TURN_B, TURN_C):
                dve.scalar_tensor_tensor(angle, turns, -part, angle, ALU.mult, ALU.add).then_inc(dve_seq, 1)
                dve.wait_ge(dve_seq, seen(dve_seq))
            dve.tensor_scalar(angle, angle, -SIN_END, SIN_END, ALU.max, ALU.min).then_inc(dve_seq, 1)
            dve.wait_ge(dve_seq, seen(dve_seq))
            dve.tensor_scalar(turns, angle, -1.0, None, ALU.mult).then_inc(dve_seq, 1)
            dve.wait_ge(dve_seq, seen(dve_seq))
            dve.tensor_tensor(place, turns, angle, ALU.min).then_inc(dve_seq, 1)
            dve.wait_ge(dve_seq, seen(dve_seq))
            dve.tensor_scalar(place, place, math.pi / 2, None, ALU.add).then_inc(dve_seq, 1)
            dve.wait_ge(dve_seq, seen(dve_seq))
            dve.tensor_scalar(turns, angle, turn_by[:, 1:2], None, ALU.mult).then_inc(dve_seq, 1)
            dve.wait_ge(dve_seq, seen(dve_seq))
            dve.sem_inc(angle_ready, 1)
            dve.wait_ge(lam_exped, seen(lam_exped))
            for layer in range(DEPTH):
                c = slice(V_NEG_LAM, V_NEG_LAM + 1)
                dve.tensor_tensor(vec[:, layer, c], lam_exp[:, 2 * layer + 1:2 * layer + 2],
                                  lam_exp[:, 2 * layer:2 * layer + 1], ALU.subtract).then_inc(dve_seq, 1)
                dve.wait_ge(dve_seq, seen(dve_seq))
                dve.tensor_tensor(vec[:, layer, c], vec[:, layer, c],
                                  vec[:, layer, V_LAM_INIT:V_LAM_INIT + 1], ALU.subtract).then_inc(dve_seq, 1)
                dve.wait_ge(dve_seq, seen(dve_seq))
                dve.tensor_tensor(vec[:, layer, V_SUBLN_SCALED:V_SUBLN_SCALED + 1],
                                  vec[:, layer, V_SUBLN:V_SUBLN + 1],
                                  vec[:, layer, V_ONE_LESS:V_ONE_LESS + 1], ALU.mult).then_inc(dve_seq, 1)
                dve.wait_ge(dve_seq, seen(dve_seq))
            seen.settle(dve)

            with dve.Fori(0, DEPTH) as layer:
                absorb()
                dve.tensor_copy(lay[:, :], vec[:, bass.ds(layer, 1), 0:LAY].rearrange("p o v -> p (o v)"))\
                   .then_inc(dve_seq, 1)
                dve.wait_ge(dve_seq, seen(dve_seq))
                dve.wait_ge(eye_in, 16)
                start_norm()
                for out, first_bank in ((q_next, PROJ), (k_next, SPARE)):
                    for n in range(2):
                        evacuate(n, out, first_bank)
                dve.sem_inc(score_free, 2)
                dve.wait_ge(tables_in, 16 * 4)
                rotate(q_next)
                rotate(k_next)
                for n in range(2):
                    evacuate(n, v_next)
                dve.sem_inc(v_ready, 1)
                split_next()
                dve.wait_ge(masks_in, 32)
                seen.settle(dve)
                with dve.Fori(0, A_UNITS):
                    unit(True)
                    seen.settle(dve)
                with dve.Fori(0, B_UNITS - 1):
                    unit(False)
                    seen.settle(dve)
                unit(False, next_attends=False)

                def gate(c, x):
                    dve.tensor_tensor(padded[:, TAPS - 1:], c, x, ALU.mult).then_inc(dve_seq, 1)
                    dve.wait_ge(dve_seq, seen(dve_seq))
                    dve.sem_inc(gate_ready, 1)

                def convolve(u, b, c):
                    conv_taps(c, lambda j: lay[:, V_CONV_MIX + TAPS * u + j:V_CONV_MIX + TAPS * u + j + 1])
                    dve.tensor_tensor(gated, b, c, ALU.mult).then_inc(dve_seq, 1)
                    dve.wait_ge(dve_seq, seen(dve_seq))

                gate(k_next[:, :], v_next[:, :])
                evacuate(0, second[0])
                convolve(0, q_next[:, :], k_next[:, :])
                dve.sem_inc(value_ready, 1)
                evacuate(1, second[0])
                keep_lo(gated)
                for out in second[1:]:
                    for n in range(2):
                        evacuate(n, out)
                gate(second[1], second[2])
                convolve(1, second[0], second[1])
                for m in range(KT):
                    add_down(m)
                dve.sem_inc(value_ready, 1)
                keep_lo(gated)
                add_last_down(layer, V_FFN_G)

                absorb()
                start_norm()

                def load_taps(at, n):
                    dve.tensor_copy(taps[:, 0:TAPS * n], lay[:, bass.ds(at, TAPS * n)]).then_inc(dve_seq, 1)
                    dve.wait_ge(dve_seq, seen(dve_seq))

                load_taps(V_CONV_FFN, 2)
                hidden(0, down=False, up_bank=SPARE)
                hidden(1)
                seen.settle(dve)
                with dve.Fori(1, F_TILES // 2) as pair:
                    load_taps(pair * (2 * TAPS) + V_CONV_FFN, 2)
                    hidden(0)
                    hidden(1)
                    seen.settle(dve)
                add_last_down(layer, V_NEXT_G)
                seen.settle(dve)

            start_norm()
            for m in range(KT):
                dve.scalar_tensor_tensor(h[:, m, :], h[:, m, :], gain[:, m:m + 1],
                                         rstd_all[:, :], ALU.mult, ALU.mult).then_inc(dve_seq, 1)
                dve.wait_ge(dve_seq, seen(dve_seq))
                dve.sem_inc(out_ready, 1)



def by_feature(a):
    return np.reshape(a, (-1, P)).T


def weight_stream(w_in, w_out, w_up, w_down):
    def projection(w, c):
        return w[:, c:c + P].reshape(KT, P, P).transpose(1, 0, 2).reshape(P, KT * P)

    a_width, b_width, c_width = A_UNITS * P, B_UNITS * P, C_UNITS * P
    units = [[0 + u * P, a_width + u * P, 2 * a_width + u * P] for u in range(A_UNITS)]
    at = 3 * a_width
    units += [[at + u * P, at + b_width + u * P, at + 2 * b_width + u * P] for u in range(B_UNITS)]
    at += 3 * b_width
    units += [[at + u * P, at + c_width + u * P, at + 2 * c_width + u * P] for u in range(C_UNITS)]
    tiles = []
    for layer in range(DEPTH):
        tiles += [projection(w_in[layer], c) for c in units[0]]
        for u in range(MIX_UNITS):
            if u + 1 < MIX_UNITS:
                tiles += [projection(w_in[layer], c) for c in units[u + 1]]
            tiles.append(w_out[layer, u * P:(u + 1) * P])
        for f in range(F_TILES):
            tiles += [projection(w_up[layer], f * P), projection(w_up[layer], D_FF + f * P)]
            if f:
                tiles.append(w_down[layer, (f - 1) * P:f * P])
        tiles.append(w_down[layer, (F_TILES - 1) * P:])
    return np.stack(tiles)


def masks_by_distance():
    d = np.arange(P)[:, None] + SEQ - P - np.arange(SEQ)[None, :]
    held = sum(((d >= 0) & (d % step == 0) & (d <= window)).astype(np.float64) for window, step in DILATED)
    causal = np.where(d >= 0, 0.0, NEG)
    dilation = np.where(held > 0, np.log(np.maximum(held, 1)) / SCALE, NEG)
    return causal, dilation.astype(np.float32)


def kernel(x, positions, norm_mix_g, w_in, lambda_q1, lambda_k1, lambda_q2, lambda_k2, subln_g, conv_mix_w,
           w_out, norm_ffn_g, w_up, conv_ffn_w, w_down, final_g):
    import concourse.bacc as bacc
    from concourse.bass_utils import run_bass_kernel_spmd
    import ml_dtypes

    (x, positions, norm_mix_g, w_in, lambda_q1, lambda_k1, lambda_q2, lambda_k2, subln_g, conv_mix_w, w_out,
     norm_ffn_g, w_up, conv_ffn_w, w_down, final_g) = (
        np.asarray(a) for a in (x, positions, norm_mix_g, w_in, lambda_q1, lambda_k1, lambda_q2, lambda_k2,
                                subln_g, conv_mix_w, w_out, norm_ffn_g, w_up, conv_ffn_w, w_down, final_g))

    vectors = np.zeros((P, DEPTH, NV), np.float32)
    for layer in range(DEPTH):
        v = vectors[:, layer]
        v[:, V_FFN_G:V_FFN_G + KT] = by_feature(norm_ffn_g[layer])
        v[:, V_NEXT_G:V_NEXT_G + KT] = by_feature(norm_mix_g[layer + 1] if layer + 1 < DEPTH else final_g)
        for j in range(TAPS):
            v[:, V_CONV_MIX + j:V_CONV_FFN:TAPS] = by_feature(conv_mix_w[layer, j])
            v[:, V_CONV_FFN + j:V_NEG_LAM:TAPS] = by_feature(conv_ffn_w[layer, j])
        v[:, V_SUBLN] = subln_g[layer]
        for n, a in enumerate((lambda_q1, lambda_k1, lambda_q2, lambda_k2)):
            v[:HEAD_DIM, V_LAMBDA + n] = a[layer]
        lam_init = 0.8 - 0.6 * math.exp(-0.3 * layer)
        v[:, V_LAM_INIT], v[:, V_ONE_LESS] = lam_init, 1.0 - lam_init

    half = ROPE_DIMS // 2
    freq = (np.float32(ROPE_THETA) ** (-(np.arange(half, dtype=np.float32) * np.float32(2.0) / ROPE_DIMS)))
    rope = np.stack([np.tile(freq, 2), np.repeat([-1.0, 1.0], half)], axis=1).astype(np.float32)
    chunks = np.reshape(positions, (1, CHUNKS, CHUNK))

    causal, dilation = masks_by_distance()
    arrays = {
        "x_t": np.ascontiguousarray(x[0].T),
        "positions": np.broadcast_to(chunks, (ROPE_DIMS, CHUNKS, CHUNK)).reshape(P, CHUNK).copy(),
        "stream": weight_stream(w_in, w_out, w_up, w_down),
        "vectors": vectors.reshape(P, DEPTH * NV),
        "first_g": np.ascontiguousarray(by_feature(norm_mix_g[0])),
        "rope": np.repeat(rope, CHUNKS, axis=0),
        "identity": np.eye(P, dtype=np.float32),
        "causal": causal.astype(ml_dtypes.bfloat16),
        "dilation": dilation,
    }
    nc = bacc.Bacc("TRN2", target_bir_lowering=False, num_devices=1)
    ins = [nc.dram_tensor(n, a.shape, mybir.dt.from_np(a.dtype), kind="ExternalInput").ap() for n, a in arrays.items()]
    out = nc.dram_tensor("out_t", (D_MODEL, SEQ), mybir.dt.float32, kind="ExternalOutput").ap()
    build(nc, *ins, out)
    result = run_bass_kernel_spmd(nc, [arrays], core_ids=[0])
    return np.ascontiguousarray(result.results[0]["out_t"].T)[None]
```
